# Optimizing a Trainium2 kernel written in Bass

```python
import math
import jax, jax.numpy as jnp
from jax import lax
import numpy as np

D_MODEL = 1024
BATCH = 1
SEQ = 256
DEPTH = 2

N_MIXERS = 2
N_POOL_LAYERS = (DEPTH + 1) // 2
N_MOBA_LAYERS = DEPTH // 2
POOL_WINDOWS = (2, 4, 8, 16)
N_POOL_GROUPS = len(POOL_WINDOWS)
POOL_GROUP = D_MODEL // N_POOL_GROUPS
HEAD_DIM = 64
N_HEADS = D_MODEL // HEAD_DIM
MOBA_BLOCK = 256
MOBA_TOPK = 3
Q_CHUNK = 128
NUM_BUCKETS = 32
MAX_DISTANCE = 1024
D_FF = 4 * D_MODEL
EPS = 1e-6


def rmsnorm(x, g):
    xf = x.astype(jnp.float32)
    y = xf * lax.rsqrt(jnp.mean(xf * xf, axis=-1, keepdims=True) + EPS)
    return (y * g.astype(jnp.float32)).astype(x.dtype)

def modulate(h, shift, scale):
    return h * (1 + scale[:, None, :]) + shift[:, None, :]

def t5_bucket(dist):
    max_exact = NUM_BUCKETS // 2
    nf = jnp.maximum(dist, 1).astype(jnp.float32)
    large = max_exact + (jnp.log(nf / max_exact) / math.log(MAX_DISTANCE / max_exact)
                         * (NUM_BUCKETS - max_exact)).astype(jnp.int32)
    large = jnp.minimum(large, NUM_BUCKETS - 1)
    return jnp.where(dist < max_exact, dist, large)

def pool_mixer(h, w_pool, pool_scale):
    B, S, D = h.shape
    hf = h.astype(jnp.float32)
    cs = jnp.concatenate([jnp.zeros((B, 1, D), jnp.float32), jnp.cumsum(hf, axis=1)], axis=1)
    t = jnp.arange(S)
    groups = []
    for g, w in enumerate(POOL_WINDOWS):
        sl = slice(g * POOL_GROUP, (g + 1) * POOL_GROUP)
        cs_g = cs[:, :, sl]
        lo = jnp.maximum(t + 1 - w, 0)
        win_sum = cs_g[:, 1:] - jnp.take(cs_g, lo, axis=1)
        cnt = jnp.minimum(t + 1, w).astype(jnp.float32)[None, :, None]
        groups.append(win_sum / cnt - hf[:, :, sl])
    pooled = jnp.stack(groups, axis=2)
    y = jnp.einsum('bsgi,gio->bsgo', pooled, w_pool.astype(jnp.float32)).reshape(B, S, D)
    return (y * pool_scale.astype(jnp.float32)).astype(h.dtype)

def moba_attention(h, w_qkv, w_o, rel_bias):
    B, S, D = h.shape
    H, Dh, BL = N_HEADS, HEAD_DIM, MOBA_BLOCK
    qkv = h @ w_qkv
    q, k, v = jnp.split(qkv, 3, axis=-1)
    q = q.reshape(B, S, H, Dh).transpose(0, 2, 1, 3)
    k = k.reshape(B, S, H, Dh).transpose(0, 2, 1, 3)
    v = v.reshape(B, S, H, Dh).transpose(0, 2, 1, 3)
    nb = -(-S // BL)
    pad = nb * BL - S
    kb = jnp.pad(k, ((0, 0), (0, 0), (0, pad), (0, 0))).reshape(B, H, nb, BL, Dh)
    vb = jnp.pad(v, ((0, 0), (0, 0), (0, pad), (0, 0))).reshape(B, H, nb, BL, Dh)
    kmean = jnp.mean(kb.astype(jnp.float32), axis=3)
    top = min(MOBA_TOPK, nb - 1)
    scale = HEAD_DIM ** -0.5
    rb = rel_bias.astype(jnp.float32)
    rbT = rb.T
    bi = jnp.arange(B)[:, None, None]
    hi = jnp.arange(H)[None, :, None]
    hi4 = jnp.arange(H)[None, :, None, None]
    n_chunks = S // Q_CHUNK

    def chunk_fn(ci):
        s0 = ci * Q_CHUNK
        qf = lax.dynamic_slice_in_dim(q, s0, Q_CHUNK, axis=2).astype(jnp.float32)
        tq = s0 + jnp.arange(Q_CHUNK)
        own = s0 // BL
        k_own = lax.dynamic_index_in_dim(kb, own, axis=2, keepdims=False)
        v_own = lax.dynamic_index_in_dim(vb, own, axis=2, keepdims=False)
        dist_own = tq[:, None] - (own * BL + jnp.arange(BL))[None, :]
        bias_own = rb[t5_bucket(jnp.maximum(dist_own, 0))].transpose(2, 0, 1)[None]
        logit_own = jnp.einsum('bhqd,bhkd->bhqk', qf, k_own.astype(jnp.float32)) * scale + bias_own
        logit_own = jnp.where((dist_own >= 0)[None, None], logit_own, -jnp.inf)
        logits = []
        sel = []
        if top > 0:
            gate = jnp.einsum('bhqd,bhnd->bhqn', qf, kmean)
            past = jnp.arange(nb) < own
            gate = jnp.where(past[None, None, None], gate, -jnp.inf)
            _, idx = lax.top_k(gate, top)
            for r in range(top):
                idx_r = idx[..., r]
                k_sel = kb[bi, hi, idx_r]
                kpos = idx_r[..., None] * BL + jnp.arange(BL)
                dist = tq[None, None, :, None] - kpos
                bias_r = rbT[hi4, t5_bucket(jnp.maximum(dist, 0))]
                lg = jnp.einsum('bhqd,bhqkd->bhqk', qf, k_sel.astype(jnp.float32)) * scale + bias_r
                lg = jnp.where((idx_r < own)[..., None], lg, -jnp.inf)
                logits.append(lg)
                sel.append(idx_r)
        logits.append(logit_own)
        p = jax.nn.softmax(jnp.concatenate(logits, axis=-1), axis=-1)
        out = jnp.einsum('bhqk,bhkd->bhqd', p[..., top * BL:], v_own.astype(jnp.float32))
        for r in range(top):
            v_sel = vb[bi, hi, sel[r]]
            out = out + jnp.einsum('bhqk,bhqkd->bhqd', p[..., r * BL:(r + 1) * BL],
                                   v_sel.astype(jnp.float32))
        return out.astype(h.dtype)

    o = lax.map(chunk_fn, jnp.arange(n_chunks))
    o = o.transpose(1, 0, 3, 2, 4).reshape(B, S, D)
    return o @ w_o

def squared_relu_mlp(h, w_up, w_down):
    a = jax.nn.relu(h @ w_up)
    return (a * a) @ w_down

def first_inputs(seed: int = 0) -> dict:
    key = jax.random.key(seed)
    ks = jax.random.split(key, 16)
    f32 = jnp.float32
    D = D_MODEL
    nrm = lambda k, shape, s: jax.random.normal(k, shape, f32) * s
    return {
        "x": nrm(ks[0], (BATCH, SEQ, D), 1.0),
        "c": nrm(ks[1], (BATCH, D), 1.0),
        "rel_bias": nrm(ks[2], (NUM_BUCKETS, N_HEADS), 0.5),
        "w_mod": nrm(ks[3], (DEPTH, D, 6 * D), 0.5 * D ** -0.5),
        "b_mod": nrm(ks[4], (DEPTH, 6 * D), 0.02),
        "norm_mix": 1.0 + nrm(ks[5], (DEPTH, D), 0.02),
        "norm_mlp": 1.0 + nrm(ks[6], (DEPTH, D), 0.02),
        "w_pool": nrm(ks[7], (N_POOL_LAYERS, N_POOL_GROUPS, POOL_GROUP, POOL_GROUP), POOL_GROUP ** -0.5),
        "pool_scale": 1.0 + nrm(ks[8], (N_POOL_LAYERS, D), 0.05),
        "w_qkv": nrm(ks[9], (N_MOBA_LAYERS, D, 3 * D), D ** -0.5),
        "w_o": nrm(ks[10], (N_MOBA_LAYERS, D, D), D ** -0.5),
        "w_up": nrm(ks[11], (DEPTH, D, D_FF), D ** -0.5),
        "w_down": nrm(ks[12], (DEPTH, D_FF, D), D_FF ** -0.5),
        "norm_final": 1.0 + nrm(ks[13], (D,), 0.02),
    }

def first_block(x, c, rel_bias, w_mod, b_mod, norm_mix, norm_mlp, w_pool, pool_scale,
              w_qkv, w_o, w_up, w_down, norm_final):
    c_act = jax.nn.silu(c)
    for i in range(DEPTH):
        mod = c_act @ w_mod[i] + b_mod[i]
        sh1, sc1, g1, sh2, sc2, g2 = jnp.split(mod, 6, axis=-1)
        h = modulate(rmsnorm(x, norm_mix[i]), sh1, sc1)
        if i % N_MIXERS == 0:
            y = pool_mixer(h, w_pool[i // N_MIXERS], pool_scale[i // N_MIXERS])
        else:
            y = moba_attention(h, w_qkv[i // N_MIXERS], w_o[i // N_MIXERS], rel_bias)
        x = x + g1[:, None, :] * y
        h = modulate(rmsnorm(x, norm_mlp[i]), sh2, sc2)
        x = x + g2[:, None, :] * squared_relu_mlp(h, w_up[i], w_down[i])
    return rmsnorm(x, norm_final)


DEPTH_2 = 1

N_META = 16
GDN_HEADS = D_MODEL // 256
GDN_DK = 128
GDN_DV = 128
FOX_HEADS = D_MODEL // 128
FOX_DH = 64
D_MIX = GDN_HEADS * GDN_DV + FOX_HEADS * FOX_DH
CONV_K = 4
CHUNK = 64
BLOCK_Q = 128
D_FF_2 = -(-8 * D_MODEL // (3 * 256)) * 256
MASK_VALUE = -1e30
GDN_QKV = 2 * GDN_HEADS * GDN_DK + GDN_HEADS * GDN_DV
IN_SIZES = (GDN_HEADS * GDN_DK, GDN_HEADS * GDN_DK, GDN_HEADS * GDN_DV, GDN_HEADS * GDN_DV,
            GDN_HEADS, GDN_HEADS,
            FOX_HEADS * FOX_DH, FOX_HEADS * FOX_DH, FOX_HEADS * FOX_DH, FOX_HEADS)
D_IN = sum(IN_SIZES)
IN_SPLITS = tuple(int(s) for s in np.cumsum(IN_SIZES)[:-1])


def rmsnorm_2(x, w):
    x32 = x.astype(jnp.float32)
    y = x32 * lax.rsqrt(jnp.mean(x32 * x32, axis=-1, keepdims=True) + EPS)
    return (y * w.astype(jnp.float32)).astype(x.dtype)

def l2norm(x):
    return x * lax.rsqrt(jnp.sum(x * x, axis=-1, keepdims=True) + EPS)

def causal_dwconv(x, w):
    k = w.shape[0]
    return lax.conv_general_dilated(x, w[:, None, :], window_strides=(1,), padding=[(k - 1, 0)],
                                    dimension_numbers=("NWC", "WIO", "NWC"),
                                    feature_group_count=x.shape[-1])

def chunk_gated_delta_rule(q, k, v, beta, g, s0, chunk):
    b, h, t, _ = q.shape
    dv = v.shape[-1]
    n = t // chunk
    q, k, v = (a.reshape(b, h, n, chunk, a.shape[-1]) for a in (q, k, v))
    beta = beta.reshape(b, h, n, chunk)
    gc = jnp.cumsum(g.reshape(b, h, n, chunk), axis=-1)
    incl = jnp.tril(jnp.ones((chunk, chunk), dtype=bool))
    strict = jnp.tril(jnp.ones((chunk, chunk), dtype=bool), -1)
    diff = gc[..., :, None] - gc[..., None, :]
    decay = jnp.where(incl, jnp.exp(jnp.where(incl, diff, 0.0)), 0.0)
    a_mat = jnp.where(strict, jnp.einsum("bhncd,bhnsd->bhncs", k, k) * decay * beta[..., :, None], 0.0)
    rhs = jnp.concatenate([v * beta[..., None], k * (beta * jnp.exp(gc))[..., None]], axis=-1)
    sol = lax.linalg.triangular_solve(a_mat + jnp.eye(chunk, dtype=a_mat.dtype), rhs,
                                      left_side=True, lower=True, unit_diagonal=True)
    u, w = sol[..., :dv], sol[..., dv:]
    qk = jnp.einsum("bhncd,bhnsd->bhncs", q, k) * decay
    xs = tuple(jnp.moveaxis(a, 2, 0) for a in (q, k, u, w, gc, qk))

    def step(state, inp):
        q_c, k_c, u_c, w_c, g_c, qk_c = inp
        v_new = u_c - jnp.einsum("bhcd,bhde->bhce", w_c, state)
        o_c = (jnp.einsum("bhcd,bhde->bhce", q_c * jnp.exp(g_c)[..., None], state)
               + jnp.einsum("bhcs,bhse->bhce", qk_c, v_new))
        g_last = g_c[..., -1:]
        state = (state * jnp.exp(g_last)[..., None]
                 + jnp.einsum("bhcd,bhce->bhde", k_c * jnp.exp(g_last - g_c)[..., None], v_new))
        return state, o_c

    s_final, o = lax.scan(step, s0, xs)
    o = jnp.moveaxis(o, 0, 2).reshape(b, h, t, dv)
    return o, s_final

def gated_deltanet_group(qkv, z, b_raw, a_raw, conv_w, a_log, dt_bias, norm_w):
    bsz, t, _ = qkv.shape
    f32 = jnp.float32
    qkv = jax.nn.silu(causal_dwconv(qkv, conv_w)).astype(f32)
    q, k, v = jnp.split(qkv, [GDN_HEADS * GDN_DK, 2 * GDN_HEADS * GDN_DK], axis=-1)
    q = l2norm(q.reshape(bsz, t, GDN_HEADS, GDN_DK)).transpose(0, 2, 1, 3) * (GDN_DK ** -0.5)
    k = l2norm(k.reshape(bsz, t, GDN_HEADS, GDN_DK)).transpose(0, 2, 1, 3)
    v = v.reshape(bsz, t, GDN_HEADS, GDN_DV).transpose(0, 2, 1, 3)
    beta = jax.nn.sigmoid(b_raw.astype(f32)).transpose(0, 2, 1)
    g = (-jnp.exp(a_log.astype(f32))
         * jax.nn.softplus(a_raw.astype(f32) + dt_bias.astype(f32))).transpose(0, 2, 1)
    s0 = jnp.zeros((bsz, GDN_HEADS, GDN_DK, GDN_DV), f32)
    o_meta, s_meta = chunk_gated_delta_rule(q[:, :, :N_META], k[:, :, :N_META], v[:, :, :N_META],
                                            beta[:, :, :N_META], g[:, :, :N_META], s0, N_META)
    o_real, _ = chunk_gated_delta_rule(q[:, :, N_META:], k[:, :, N_META:], v[:, :, N_META:],
                                       beta[:, :, N_META:], g[:, :, N_META:], s_meta, CHUNK)
    o = jnp.concatenate([o_meta, o_real], axis=2).transpose(0, 2, 1, 3)
    zg = jax.nn.silu(z.astype(f32).reshape(bsz, t, GDN_HEADS, GDN_DV))
    o = o * lax.rsqrt(jnp.mean(o * o, axis=-1, keepdims=True) + EPS) * norm_w.astype(f32) * zg
    return o.reshape(bsz, t, GDN_HEADS * GDN_DV).astype(qkv.dtype)

def forgetting_attention_group(q, k, v, f_raw, f_bias):
    bsz, t, _ = q.shape
    f32 = jnp.float32
    q, k, v = (a.astype(f32).reshape(bsz, t, FOX_HEADS, FOX_DH) for a in (q, k, v))
    logf = jax.nn.log_sigmoid(f_raw.astype(f32) + f_bias.astype(f32))
    c = jnp.cumsum(logf, axis=1).transpose(0, 2, 1)
    scale = FOX_DH ** -0.5
    n_blocks = (t - N_META) // BLOCK_Q
    bounds = [0, N_META] + [N_META + (i + 1) * BLOCK_Q for i in range(n_blocks)]
    outs = []
    for s, e in zip(bounds[:-1], bounds[1:]):
        sc = (jnp.einsum("bqhd,bkhd->bhqk", q[:, s:e], k[:, :e]) * scale
              + c[:, :, s:e, None] - c[:, :, None, :e])
        causal = jnp.arange(s, e)[:, None] >= jnp.arange(e)[None, :]
        p = jax.nn.softmax(jnp.where(causal, sc, MASK_VALUE), axis=-1)
        outs.append(jnp.einsum("bhqk,bkhd->bqhd", p, v[:, :e]))
    return jnp.concatenate(outs, axis=1).reshape(bsz, t, FOX_HEADS * FOX_DH)

def swiglu(x, w_gate, w_up, w_down):
    return (jax.nn.silu(x @ w_gate) * (x @ w_up)) @ w_down

def second_inputs(seed: int = 0) -> dict:
    key = jax.random.key(seed)
    ks = jax.random.split(key, 15)
    nrm = jax.random.normal
    dt = jnp.exp(jax.random.uniform(ks[6], (DEPTH_2, GDN_HEADS), minval=math.log(1e-3), maxval=math.log(1e-1)))
    return {
        "x": nrm(ks[0], (BATCH, SEQ, D_MODEL), jnp.float32),
        "meta_tokens": nrm(ks[1], (N_META, D_MODEL), jnp.float32),
        "attn_norm_w": 1.0 + 0.02 * nrm(ks[2], (DEPTH_2, D_MODEL), jnp.float32),
        "w_in": nrm(ks[3], (DEPTH_2, D_MODEL, D_IN), jnp.float32) * D_MODEL ** -0.5,
        "conv_w": nrm(ks[4], (DEPTH_2, CONV_K, GDN_QKV), jnp.float32) * CONV_K ** -0.5,
        "a_log": jnp.log(jax.random.uniform(ks[5], (DEPTH_2, GDN_HEADS), minval=1.0, maxval=16.0)),
        "dt_bias": dt + jnp.log(-jnp.expm1(-dt)),
        "gdn_norm_w": 1.0 + 0.02 * nrm(ks[7], (DEPTH_2, GDN_DV), jnp.float32),
        "fgate_b": 2.0 + 0.5 * nrm(ks[8], (DEPTH_2, FOX_HEADS), jnp.float32),
        "w_out": nrm(ks[9], (DEPTH_2, D_MIX, D_MODEL), jnp.float32) * D_MIX ** -0.5,
        "ffn_norm_w": 1.0 + 0.02 * nrm(ks[10], (DEPTH_2, D_MODEL), jnp.float32),
        "w_gate": nrm(ks[11], (DEPTH_2, D_MODEL, D_FF_2), jnp.float32) * D_MODEL ** -0.5,
        "w_up": nrm(ks[12], (DEPTH_2, D_MODEL, D_FF_2), jnp.float32) * D_MODEL ** -0.5,
        "w_down": nrm(ks[13], (DEPTH_2, D_FF_2, D_MODEL), jnp.float32) * D_FF_2 ** -0.5,
        "final_norm_w": 1.0 + 0.02 * nrm(ks[14], (D_MODEL,), jnp.float32),
    }

def second_block(x, meta_tokens, attn_norm_w, w_in, conv_w, a_log, dt_bias, gdn_norm_w, fgate_b,
              w_out, ffn_norm_w, w_gate, w_up, w_down, final_norm_w):
    bsz = x.shape[0]
    meta = jnp.broadcast_to(meta_tokens[None].astype(x.dtype), (bsz, N_META, D_MODEL))
    h = jnp.concatenate([meta, x], axis=1)
    for l in range(DEPTH_2):
        u = rmsnorm_2(h, attn_norm_w[l])
        proj = u @ w_in[l]
        gq, gk, gv, gz, gb, ga, fq, fk, fv, ff = jnp.split(proj, IN_SPLITS, axis=-1)
        o_gdn = gated_deltanet_group(jnp.concatenate([gq, gk, gv], axis=-1), gz, gb, ga,
                                     conv_w[l], a_log[l], dt_bias[l], gdn_norm_w[l])
        o_fox = forgetting_attention_group(fq, fk, fv, ff, fgate_b[l]).astype(h.dtype)
        h = h + jnp.concatenate([o_gdn, o_fox], axis=-1) @ w_out[l]
        h = h + swiglu(rmsnorm_2(h, ffn_norm_w[l]), w_gate[l], w_up[l], w_down[l])
    h = rmsnorm_2(h, final_norm_w)
    return h[:, N_META:]


def setup_inputs(seed=0):
    out = dict(first_inputs(seed))
    for name, value in second_inputs(seed + 1).items():
        if name != "x":
            out[name + "_2"] = value
    return out


def reference(
    x, c, rel_bias, w_mod, b_mod, norm_mix, norm_mlp, w_pool, pool_scale, w_qkv, w_o, w_up,
    w_down, norm_final, meta_tokens_2, attn_norm_w_2, w_in_2, conv_w_2, a_log_2, dt_bias_2,
    gdn_norm_w_2, fgate_b_2, w_out_2, ffn_norm_w_2, w_gate_2, w_up_2, w_down_2, final_norm_w_2,
):
    x = first_block(
        x, c, rel_bias, w_mod, b_mod, norm_mix, norm_mlp, w_pool, pool_scale, w_qkv, w_o, w_up,
        w_down, norm_final,
    )
    return second_block(
        x, meta_tokens_2, attn_norm_w_2, w_in_2, conv_w_2, a_log_2, dt_bias_2, gdn_norm_w_2,
        fgate_b_2, w_out_2, ffn_norm_w_2, w_gate_2, w_up_2, w_down_2, final_norm_w_2,
    )


_drawn_inputs = setup_inputs


def setup_inputs(seed=0):
    import zlib

    import numpy as np

    out = dict(_drawn_inputs(seed))
    spreads = {}
    factors = {'norm_mix': 6.763,
     'norm_mlp': 3.533,
     'pool_scale': 3.283,
     'attn_norm_w_2': 3.532,
     'gdn_norm_w_2': 22.208,
     'ffn_norm_w_2': 12.621,
     'final_norm_w_2': 23.117,
     'fgate_b_2': 2.99}
    for name, (base, spread) in spreads.items():
        noise = np.random.default_rng([zlib.crc32(name.encode()), seed]).standard_normal(out[name].shape)
        drawn = base * np.exp(spread * noise) if base else spread * noise
        out[name] = __import__('jax').numpy.asarray(drawn.astype(out[name].dtype))
    for name, factor in factors.items():
        out[name] = (out[name] * factor).astype(out[name].dtype)
    return out
```

```python
import math
from contextlib import ExitStack

import numpy as np

import concourse.bass as bass
from concourse import mybir

F32 = mybir.dt.float32
F32R = mybir.dt.float32r
ALU = mybir.AluOpType
ACT = mybir.ActivationFunctionType
AX_X = mybir.AxisListType.X

P = 128
SEQ = 256
NM = SEQ // P
D = 1024
KD = D // P
META = 16
TT = META + SEQ
EPS = 1e-6
NEG = -1e30

R = 4
SLOT = 4096
HALF = SLOT // 2
PIECE = HALF // 2

MOD_SECTIONS = 6
NJ = 8
HEADS, DH = 16, 64
BUCKETS = 32
FH = 8
GH = 4
FF2 = 2816
NJ2 = FF2 // 256
NDIST = 384

N_POOL, N_MLP0, N_QKV, N_WO, N_MOD1, N_WO1, N_MLP1 = 4, 11, 41, 47, 48, 56, 57
MOD0_LOADS = [0, 1, 2, 3, 5, 6, 7, 8, 9, 10, 12, 13]
MOD0_PE = [2] * 4 + [3] * 6 + [0] * 2
NMU, MUW = 8, 384
T_POOL, T_MLP0, T_QKV, T_WO, T_MLP1 = 0, 1, 17, 23, 25
N_WIN, T_WIN = 73, 41
N_WOUT, T_WOUT = 80, 48
N_FFN, T_FFN = 82, 50
PASSES = [(0, 0), (0, 1), (1, 0)]


def landed(n):
    return n % R, 16 * (n // R + 1)


def build(nc, a, out):
    ctx = ExitStack()
    with ctx:
        def sb(name, shape, dt=F32):
            return ctx.enter_context(nc.sbuf_tensor(name, shape, dt))

        def sem(name):
            return ctx.enter_context(nc.semaphore(name))

        raw = sb("raw", [P, R, SLOT])
        w_at = nc.sbuf_base
        wh = sb("wh", [P, 2, HALF], F32R)
        wl = sb("wl", [P, 2, HALF], F32R)
        x = sb("x", [P, NM, D])
        f_at = nc.sbuf_base
        hf = sb("hf", [P, KD, TT])
        H = sb("H", [P, KD, TT], F32R)
        L = sb("L", [P, KD, TT], F32R)
        gate = [sb(f"gate{i}", [P, D]) for i in range(2)]
        ident = sb("ident", [P, P])
        ones = sb("ones", [P, P])
        prow = sb("prow", [P, 2, P])
        pcol = sb("pcol", [P, 2, P])
        wtri = sb("wtri", [P, META + P + TT])
        alog = sb("alog", [P, GH])
        dtb = sb("dtb", [P, GH])
        fgb = sb("fgb", [P, FH])
        gnorm = sb("gnorm", [P, P])
        wsm = sb("wsm", [P, KD, 16])
        sm = sb("sm", [P, 3, 16])
        tks = sb("tks", [P, 4, 3, 12])
        beta = sb("beta", [P, 3, 4])
        eb = sb("eb", [P, 2, 3, 4])
        nega = sb("nega", [P, 2, 4])
        gdec = sb("gdec", [P, 3, 4])
        EG = sb("EG", [P, 3, 12])
        nrm = sb("nrm", [P, 3, 2, 3, 4])
        coef = sb("coef", [P, 4, 3, 4])
        onrm = sb("onrm", [P, 3, 2, 4])
        epsq = sb("epsq", [P, 1])
        ccol = sb("ccol", [P, 5, KD])
        modc = sb("modc", [P, 2, 48])
        mods = sb("mods", [P, 6, KD])
        stat = sb("stat", [P, 8, 4])
        inv16 = sb("inv16", [P, 16])
        epsc = sb("epsc", [P, 1])
        rb = sb("rb", [BUCKETS + 1, HEADS])
        rsum = sb("rsum", [P, 32])
        rrec = sb("rrec", [P, 32])
        AK = 60 * 1024
        arena_at = (nc.sbuf_base + 31) // 32 * 32
        arena = sb("arena", [P, AK // 4])

        def at(name, off_k, shape, dt=F32):
            n = int(np.prod(shape[1:]))
            w0 = int(off_k * 256)
            v = arena[0:shape[0], w0:w0 + n]
            if dt is not F32:
                v = v.bitcast(dt)
            if len(shape) == 3:
                v = v.rearrange("p (a b) -> p a b", a=shape[1])
            if len(shape) == 4:
                v = v.rearrange("p (a b c) -> p a b c", a=shape[1], b=shape[2])
            return v

        def fixed(base, name, off_k, shape):
            return nc.alloc_sbuf_tensor_at(name, shape, F32, offset=base + int(off_k * 1024))
        tok = at("tok", 0, [P, NM, D])
        relu = at("relu", 8, [P, NM, 512])
        act = at("act", 12, [P, NM, 512])
        zrow = sb("zrow", [1, P], mybir.dt.bfloat16)
        aTh = nc.alloc_sbuf_tensor_at("aTh", [P, 4, SEQ], F32R, offset=arena_at + 16 * 1024)
        aTl = nc.alloc_sbuf_tensor_at("aTl", [P, 4, SEQ], F32R, offset=arena_at + 20 * 1024)
        acc = at("acc", 48, [P, 2, 512])
        accu = fixed(f_at, "accu", 0, [P, NMU, MUW])
        win = [at("win0", 8, [P, KD, TT]), at("win1", 17, [P, KD, TT])]
        TB = at("TB", 28, [P, HEADS, SEQ])
        diag = at("diag", 52, [P, KD, P])
        oh = at("oh", 44, [BUCKETS + 1, NDIST])
        ftab = at("ftab", 46, [HEADS, NDIST])
        qT = at("qT", 44, [P, KD, SEQ])
        kT = at("kT", 52, [P, KD, SEQ])
        v_tok = at("v_tok", 8, [P, NM, D])
        t_sc = at("t_sc", 16, [P, 4, 384])
        P_sc = at("P_sc", 22, [P, 2, 384])
        PT_sc = at("PT_sc", 25, [P, 2, 384])

        xm = at("xm", 28, [META, D])
        tokm = at("tokm", 32, [META, D])
        gT = at("gT", 8, [P, 12, TT + 3])
        yT = at("yT", 21.5, [P, 12, TT])
        fT = at("fT", 34.5, [P, 12, TT])
        zs = at("zs", 47.5, [P, NM, 512])
        masks = gate[0][:, :].rearrange("p (l c) -> p l c", l=8)
        ncT = at("ncT", 58, [FH, TT])
        cm0 = fixed(f_at, "cm0", 0, [P, FH, META + P])
        cm1 = fixed(f_at, "cm1", 4.75, [P, FH, TT])
        vt = at("vt", 8, [P, NM, 512])
        vtm = at("vtm", 12, [META, 512])
        t_f = at("t_f", 14, [P, 2, 416])
        P_f = at("P_f", 17.5, [P, 2, 416])
        PTa = at("PTa", 52, [P, 2, 384])
        PTb = at("PTb", 55.5, [META, 2, 256])
        rf = rsum
        q_t = fixed(f_at, "q_t", 0, [P, NM, GH, P])
        k_t = fixed(f_at, "k_t", 4, [P, NM, GH, P])
        v_t = fixed(f_at, "v_t", 8, [P, NM, GH, P])
        kv_m = fixed(f_at, "kv_m", 12, [META, 2, GH, P])
        AT = fixed(f_at, "AT", 16, [P, NM, GH, P])
        PT = fixed(f_at, "PT", 20, [P, NM, GH, P])
        Al = fixed(f_at, "Al", 0, [P, NM, GH, P])
        X = fixed(f_at, "X", 4, [P, NM, GH, P])
        u = fixed(f_at, "u", 8, [P, NM, GH, P])
        wT = fixed(f_at, "wT", 12, [P, NM, GH, P])
        Kn = fixed(w_at, "Kn", 0, [P, NM, GH, P])
        Kb = fixed(w_at, "Kb", 4, [P, NM, GH, P])
        Qn = fixed(w_at, "Qn", 8, [P, NM, GH, P])
        Qg = fixed(w_at, "Qg", 12, [P, NM, GH, P])
        Knm = fixed(w_at, "Knm", 16, [META, GH, P])
        Kbm = fixed(w_at, "Kbm", 18, [META, GH, P])
        R1m = fixed(w_at, "R1m", 20, [META, GH, P])
        Kdm = fixed(w_at, "Kdm", 22, [META, GH, P])
        DL = fixed(w_at, "DL", 24, [P, NM, GH, P])
        E_ = fixed(w_at, "E_", 28, [P, NM, GH, P])
        junk = fixed(w_at, "junk", 0, [P, 20, P])
        junk_o = fixed(f_at, "junk_o", 0, [P, NM * GH, P])
        Kd = at("Kd", 8, [P, NM, GH, P])
        R1 = at("R1", 12, [P, NM, GH, P])
        R2 = at("R2", 16, [P, NM, GH, P])
        KnT = at("KnT", 20, [P, NM, GH, P])
        KbT = at("KbT", 24, [P, NM, GH, P])
        QnT = at("QnT", 28, [P, NM, GH, P])
        QgT = at("QgT", 34.5, [P, NM, GH, P])
        T_ = at("T_", 38.5, [P, NM, GH, P])
        TT_ = at("TT_", 42.5, [P, NM, GH, P])
        Sst = at("Sst", 52, [P, GH, P])
        vn = at("vn", 54, [P, GH, P])
        um = at("um", 56, [META, GH, P])
        small = [at(f"small{i}", 58 + 0.25 * i, [P, GH, META]) for i in range(8)]
        KnTm, KbTm, DLm, Em, ATm, Alm, Tm, Xm = small
        TTm = at("TTm", 33, [META, GH, META])

        ps = ctx.enter_context(nc.psum_tensor("ps", [P, 8, 512], F32))

        scratch = nc.dram_tensor("bias_rows", [HEADS, NDIST], F32).ap()

        raw_in = [sem(f"raw_in{i}") for i in range(R)]
        NAMES = """x_in c_in cc_set mod_accb mod_accu nk_sq pg_set par_in rb_in oh_in f_out tb_in made ptr pcopied c_e
            c_s mod_chain mod_acc mod_mm mod_col split_h split_l split_used gate_diag gate_mm gate_set mods_set
            f_mm f_sb sq_done rstd_done xn_done tr_done hf_done hs_h hs_l sc_chain pool_chain res_mul res_add
            res_add1 y_done u_done r_done a_done t_done th_done tl_done qkv_mm ev_act ev_dve s_mm t_set p_set
            pt_mm pt_ev o_mm o_ev rec_set out_st row_in xm_in sqm_done par2_in wsm_in mask_in made2 xp_done
            xnm_done mtr_done hfm_done sm_mm sm_set pj_mm pj_ev cv_ev vtm_ev nrm_sq on_sq conv silu_set tk_d tk_a
            nc_mm nc_set gs_mm gs_set bc_mm cm_raw cm_set vt_mm vt_ev og_set fs_mm ft_set fp_set fpt_mm fpa_ev
            fpb_ev fo_mm fo_ev gt_mm gt_d gt_a nrm_a coef_d sc_d sc_p dl_p d_mm e_set tt_mm tt_d tt_a kk_mm at_d
            at_p t0_set t0_mm t0_ev al_p x_mm x_ev z_mm t_up uw_mm u_ev w_ev s1_mm ws_mm vn_set go_mm ds_mm s_set
            on_set oz_set r2_add gu_done gr_done ga_done gt_done gth_done gtl_done fin_set"""
        S = {n: sem(n) for n in NAMES.split()}

        wmod = [a["w_mod"][l].rearrange("(k p) n -> p k n", p=P) for l in range(2)]
        wup = [a["w_up"][l].rearrange("(k p) n -> p k n", p=P) for l in range(2)]
        wdn = [a["w_down"][l].rearrange("(j k p) n -> j p k n", p=P, k=4) for l in range(2)]
        wpool = a["w_pool"][0].rearrange("g (k p) n -> p g k n", p=P)
        wqkv = a["w_qkv"][0].rearrange("(k p) n -> p k n", p=P)
        wo = a["w_o"][0].rearrange("(k p) n -> p k n", p=P)

        win_w = a["w_in_2"][0].rearrange("(k p) n -> p k n", p=P)
        wout = a["w_out_2"][0].rearrange("(k p) n -> p k n", p=P)
        wgate = a["w_gate_2"][0].rearrange("(k p) n -> p k n", p=P)
        wup2 = a["w_up_2"][0].rearrange("(k p) n -> p k n", p=P)
        wdn2 = a["w_down_2"][0].rearrange("(j k p) n -> j p k n", p=P, k=2)
        WIN_COLS = [0, 512, 1024, 1536, 2056, 2568, 3080]

        def before(n):
            return 16 * len([i for i in range(N_FFN) if i % R == n % R])

        def kview(s):
            return raw[:, s, :].rearrange("p (k n) -> p k n", k=KD)

        def dview(s):
            return raw[:, s, :].rearrange("p (k n) -> p k n", k=4)

        def groups(lv):
            return range(3) if lv <= 3 else range(2)

        def count(lv, g):
            return sum(len(groups(i)) for i in range(1, lv)) + g

        block = ctx.enter_context(nc.Block())

        @block.sync
        def _(e):
            e.dma_start(prow[0:8, 1, :], a["c"].rearrange("b (r p) -> (b r) p", p=P)).then_inc(S["c_in"], 16)

            def load(slot, view, src):
                e.dma_start(view, src).then_inc(raw_in[slot], 16)

            def free_split(t):
                e.wait_ge(S["split_l"], 4 * t + 4)

            def load_mod0(u):
                n = MOD0_LOADS[u]
                if n >= R and n != 8:
                    e.wait_ge(S["mod_mm"], MOD0_LOADS.index(n - R) + 1)
                load(n % R, kview(n % R), wmod[0][:, :, 512 * u:512 * u + 512])

            load_mod0(0)
            e.dma_start(prow[0:96, 0, :], a["b_mod"].rearrange("l (r p) -> (l r) p", p=P)).then_inc(S["par_in"], 16)
            e.dma_start(prow[96:112, 0, :], a["norm_mix"].rearrange("l (r p) -> (l r) p", p=P)).then_inc(S["par_in"], 16)
            e.dma_start(prow[112:128, 0, :], a["norm_mlp"].rearrange("l (r p) -> (l r) p", p=P)).then_inc(S["par_in"], 16)
            e.dma_start(prow[8:16, 1, :], a["pool_scale"].rearrange("b (r p) -> (b r) p", p=P)).then_inc(S["par_in"], 16)
            e.dma_start(prow[16:24, 1, :], a["attn_norm_w_2"].rearrange("b (r p) -> (b r) p", p=P)).then_inc(S["par_in"], 16)
            e.dma_start(prow[24:32, 1, :], a["ffn_norm_w_2"].rearrange("b (r p) -> (b r) p", p=P)).then_inc(S["par_in"], 16)
            e.dma_start(prow[32:80, 1, :], a["conv_w_2"][0].rearrange("j (r p) -> (j r) p", p=P)).then_inc(S["par_in"], 16)
            e.dma_start(rb[0:BUCKETS, :], a["rel_bias"]).then_inc(S["rb_in"], 16)
            e.dma_start(oh[:, :], a["onehot"]).then_inc(S["oh_in"], 16)
            load_mod0(1)
            e.dma_start(x[:, :, :], a["x"][0].rearrange("(m p) d -> p m d", p=P)).then_inc(S["x_in"], 16)
            load_mod0(2)
            load_mod0(3)
            e.wait_ge(S["mod_mm"], 1)
            load(0, raw[:, 0, 0:HALF].rearrange("p (g k n) -> p g k n", g=4, k=2), wpool)
            for u in range(4, 10):
                if u == 7:
                    free_split(T_POOL)
                load_mod0(u)
            e.wait_ge(S["mod_mm"], 7)
            load(N_MLP0 % R, kview(N_MLP0 % R), wup[0][:, :, 0:512])
            load_mod0(10)
            e.wait_ge(S["mod_mm"], 10)
            load(2, kview(2), wup[0][:, :, 512:1024])
            load_mod0(11)
            free_split(T_MLP0)
            load(3, dview(3), wdn[0][0])

            def load_mod1(slot, cols):
                load(slot, kview(slot)[:, :, 0:256], wmod[1][:, :, cols])
            with e.Fori(2, 8) as j:
                free_split(T_MLP0 + 1 + 2 * (j - 2))
                load(2, kview(2), wup[0][:, :, bass.ds(512 * j, 512)])
                free_split(T_MLP0 + 2 + 2 * (j - 2))
                load(3, dview(3), wdn[0][bass.ds(j - 1, 1)].rearrange("a p k n -> (a p) k n"))
                for r in range(2):
                    e.wait_ge(S[("mod_acc", "mod_accb")[r]], (9, -1)[r] + j)
                    load_mod1(r, bass.ds(512 * (j - 2) + 256 * r, 256))
            e.wait_ge(S["mod_acc"], 17)
            load(0, dview(0), wdn[0][7])
            e.wait_ge(S["mod_accb"], 7)
            load(1, kview(1), wqkv[:, :, 0:512])
            for i in range(1, 7):
                free_split(T_QKV + i - 4)
                src = wqkv[:, :, 512 * i:512 * i + 512] if i < 6 else wo[:, :, 0:512]
                load((N_QKV + i) % R, kview((N_QKV + i) % R), src)
            for u in range(NMU):
                if u < R:
                    free_split(T_QKV + 3 + u)
                else:
                    e.wait_ge(S["mod_accu"], u - R + 1)
                s = (N_MOD1 + u) % R
                load(s, raw[:, s, 0:KD * MUW].rearrange("p (k n) -> p k n", k=KD),
                     wmod[1][:, :, 3 * D + MUW * u:3 * D + MUW * u + MUW])
            e.wait_ge(S["mod_accu"], 5)
            load(N_WO1 % R, kview(N_WO1 % R), wo[:, :, 512:1024])
            e.wait_ge(S["mod_accu"], 6)
            load(1, kview(1), wup[1][:, :, 0:512])
            e.wait_ge(S["mod_accu"], NMU)
            with e.Fori(0, 3) as i:
                for r in range(2):
                    free_split(T_MLP1 - 3 + 4 * i + 2 * r)
                    s = (N_MLP1 + 1 + 2 * r) % R
                    load(s, kview(s), wup[1][:, :, bass.ds(512 * (2 * i + 1 + r), 512)])
                    free_split(T_MLP1 - 2 + 4 * i + 2 * r)
                    s = (N_MLP1 + 2 + 2 * r) % R
                    load(s, dview(s), wdn[1][bass.ds(2 * i + r, 1)].rearrange("a p k n -> (a p) k n"))
            free_split(T_MLP1 + 9)
            load(2, kview(2), wup[1][:, :, 512 * 7:512 * 8])
            free_split(T_MLP1 + 10)
            load(3, dview(3), wdn[1][6])
            free_split(T_MLP1 + 11)
            load(0, dview(0), wdn[1][7])
            for i in range(9):
                if i == 0:
                    e.wait_ge(S["res_mul"], 12)
                    e.dma_start(gate[0][:, :], a["norm_final"].partition_broadcast(P)).then_inc(S["row_in"], 16)
                    e.wait_ge(S["t_set"], 2 * HEADS)
                    e.dma_start(xm, a["meta_tokens_2"]).then_inc(S["xm_in"], 16)
                free_split(T_WIN + i - 4)
                src = win_w[:, :, WIN_COLS[i]:WIN_COLS[i] + 512] if i < 7 else wout[:, :, 512 * (i - 7):512 * (i - 6)]
                load((N_WIN + i) % R, kview((N_WIN + i) % R), src)
            e.wait_ge(S["xp_done"], 2)
            e.dma_start(masks[:, 0:7, :], a["level_masks"]).then_inc(S["mask_in"], 16)
            e.wait_ge(S["res_mul"], 16)
            e.dma_start(gate[1][:, :], a["final_norm_w_2"].partition_broadcast(P)).then_inc(S["row_in"], 16)

            def load_g(slot, cols):
                v = kview(slot)
                load(slot, v[:, :, 0:256], wgate[:, :, cols])
                load(slot, v[:, :, 256:512], wup2[:, :, cols])

            def load_d(slot, src):
                load(slot, raw[:, slot, 0:HALF].rearrange("p (k n) -> p k n", k=2), src)
            free_split(T_FFN - 4)
            load_g(N_FFN % R, slice(0, 256))
            for r in range(2):
                j = 1 + r
                free_split(T_FFN - 3 + 2 * r)
                load_g((N_FFN + 1 + 2 * r) % R, slice(256 * j, 256 * j + 256))
                free_split(T_FFN - 2 + 2 * r)
                load_d((N_FFN + 2 + 2 * r) % R, wdn2[j - 1])
            with e.Fori(1, 5) as i:
                for r in range(2):
                    free_split(T_FFN - 3 + 2 * r + 4 * i)
                    load_g((N_FFN + 1 + 2 * r) % R, bass.ds(512 * i + 256 * (1 + r), 256))
                    free_split(T_FFN - 2 + 2 * r + 4 * i)
                    load_d((N_FFN + 2 + 2 * r) % R, wdn2[bass.ds(2 * i + r, 1)].rearrange("a p k n -> (a p) k n"))
            free_split(T_FFN + 17)
            load_d((N_FFN + 21) % R, wdn2[NJ2 - 1])
            for m in range(NM):
                e.wait_ge(S["fin_set"], m + 1)
                e.dma_start(out[0, P * m:P * m + P, :], tok[:, m, :]).then_inc(S["out_st"], 16)
            e.wait_ge(S["out_st"], 16 * NM)

        @block.gpsimd
        def _(e):
            e.memset(ident[:, :], 0.0).then_inc(S["made"], 1)
            e.memset(ones[:, :], 1.0).then_inc(S["made"], 1)
            e.wait_ge(S["made"], 2)
            e.affine_select(out=ident[:, :], in_=ident[:, :], compare_op=ALU.not_equal, fill=1.0, base=0,
                            pattern=[[-1, P]], channel_multiplier=1).then_inc(S["made"], 1)
            e.iota(inv16[:, :], [[1, 16]], base=1, channel_multiplier=0,
                   allow_small_or_imprecise_dtypes=True).then_inc(S["made"], 1)
            e.memset(zrow[:, :], 0.0).then_inc(S["made"], 1)
            e.memset(epsc[:, :], EPS).then_inc(S["made"], 1)
            e.wait_ge(S["made"], 6)
            e.memset(rb[BUCKETS:BUCKETS + 1, :], NEG).then_inc(S["made"], 1)
            e.wait_ge(S["f_sb"], 1)
            e.dma_start(scratch, ftab[:, :]).then_inc(S["f_out"], 16)
            e.wait_ge(S["f_out"], 16)
            e.dma_start(TB, bass.AP(tensor=scratch.tensor, offset=0, ap=[[1, P], [NDIST, HEADS], [1, SEQ]])
                        ).then_inc(S["tb_in"], 16)
            e.memset(wtri[:, :], 1.0).then_inc(S["made2"], 1)
            e.memset(sm[:, :, :], 0.0).then_inc(S["made2"], 1)
            e.memset(EG[:, :, :], 1.0).then_inc(S["made2"], 1)
            e.memset(nrm[:, :, :, :, :], 1.0).then_inc(S["made2"], 1)
            e.memset(epsq[:, :], EPS * P).then_inc(S["made2"], 1)
            e.wait_ge(S["made2"], 1)
            e.affine_select(out=wtri[:, :], in_=wtri[:, :], compare_op=ALU.is_ge, fill=0.0, base=-(META + P),
                            pattern=[[1, META + P + TT]], channel_multiplier=-1).then_inc(S["made2"], 1)
            for dst, name in ((alog, "a_log_2"), (dtb, "dt_bias_2"), (fgb, "fgate_b_2"), (gnorm, "gdn_norm_w_2")):
                e.dma_start(dst[:, :], a[name][0].partition_broadcast(P)).then_inc(S["par2_in"], 16)
            e.dma_start(wsm[:, :, 0:8], win_w[:, :, 2048:2056]).then_inc(S["wsm_in"], 16)
            e.dma_start(wsm[:, :, 8:16], win_w[:, :, 3592:3600]).then_inc(S["wsm_in"], 16)
            nres = [0]

            def residual():
                i = nres[0]
                nres[0] += 1
                for c in range(2):
                    e.wait_ge(S["res_mul"], 4 * i + c + 1)
                    e.tensor_tensor(x[:, 0, 512 * c:512 * c + 512], x[:, 0, 512 * c:512 * c + 512],
                                    tok[:, 0, 512 * c:512 * c + 512], ALU.add).then_inc(S["res_add"], 1)
            e.wait_ge(S["x_in"], 16)
            residual()

            def squares(it):
                for m in range(NM):
                    e.wait_ge(S["r_done"], 2 * it + m + 1)
                    e.tensor_tensor(act[:, m, :], relu[:, m, :], relu[:, m, :], ALU.mult).then_inc(S["a_done"], 1)
            squares(0)
            with e.Fori(1, 8) as j:
                squares(j)
            residual()
            residual()
            squares(8)
            with e.Fori(9, 16) as j:
                squares(j)
            residual()
            e.wait_ge(S["split_used"], 2 * T_WIN)
            e.memset(gT[:, :, 0:3], 0.0).then_inc(S["made2"], 1)
            e.wait_ge(S["xp_done"], 2)
            e.memset(masks[:, 7, :], 1.0).then_inc(S["made2"], 1)
            e.wait_ge(S["made2"], 8)
            e.affine_select(out=masks[:, 7, :], in_=masks[:, 7, :], compare_op=ALU.is_gt, fill=0.0, base=0,
                            pattern=[[-1, P]], channel_multiplier=1).then_inc(S["made2"], 1)
            e.wait_ge(S["made2"], 9)
            for i in range(2):
                hs = slice(4 * i, 4 * i + 4)
                e.wait_ge(S["cm_raw"], 4 * i + 4)
                e.affine_select(out=cm0[:, hs, :], in_=cm1[:, hs, 0:META + P], compare_op=ALU.is_ge, fill=NEG, base=META,
                                pattern=[[0, 4], [-1, META + P]], channel_multiplier=1).then_inc(S["cm_set"], 1)
                e.wait_ge(S["cm_set"], 2 * i + 1)
                e.affine_select(out=cm1[:, hs, :], in_=cm1[:, hs, :], compare_op=ALU.is_ge, fill=NEG, base=META + P,
                                pattern=[[0, 4], [-1, TT]], channel_multiplier=1).then_inc(S["cm_set"], 1)
            e.wait_ge(S["silu_set"], 4)
            for m in range(NM):
                e.tensor_tensor(zs[:, m, :].rearrange("p (h d) -> p h d", h=GH), zs[:, m, :].rearrange("p (h d) -> p h d", h=GH),
                                gnorm[:, :].unsqueeze(1).broadcast_to([P, GH, P]), ALU.mult).then_inc(S["oz_set"], 1)

            def bc(col, n, w):
                return col.unsqueeze(2).broadcast_to([n, GH, w])
            e.wait_ge(S["tk_d"], 8)
            e.wait_ge(S["nrm_a"], 2)
            for m in range(NM):
                e.tensor_tensor(DL[:, m, :, :], masks[:, 7, :].unsqueeze(1).broadcast_to([P, GH, P]),
                                bc(gdec[:, 1 + m, :], P, P), ALU.mult).then_inc(S["dl_p"], 1)
            e.tensor_tensor(DLm[0:META], masks[0:META, 7, 0:META].unsqueeze(1).broadcast_to([META, GH, META]),
                            bc(gdec[0:META, 0, :], META, META), ALU.mult).then_inc(S["dl_p"], 1)
            e.wait_ge(S["gt_a"], 4)
            e.wait_ge(S["gt_d"], 4)
            e.wait_ge(S["coef_d"], 3)
            for m in range(NM):
                e.tensor_tensor(R1[:, m], v_t[:, m], bc(beta[:, 1 + m, :], P, P), ALU.mult).then_inc(S["sc_p"], 1)
            e.tensor_tensor(R1m[:, :, :], kv_m[:, 1], bc(beta[0:META, 0, :], META, P), ALU.mult).then_inc(S["sc_p"], 1)
            e.tensor_tensor(Kdm[:, :, :], kv_m[:, 0], bc(coef[0:META, 2, 0, :], META, P), ALU.mult).then_inc(S["sc_p"], 1)
            for m in range(NM):
                e.tensor_tensor(R2[:, m], k_t[:, m], bc(coef[:, 1, 1 + m, :], P, P), ALU.mult).then_inc(S["sc_p"], 1)
                e.tensor_tensor(Kd[:, m], k_t[:, m], bc(coef[:, 2, 1 + m, :], P, P), ALU.mult).then_inc(S["sc_p"], 1)

            order = [(0, ALU.is_gt), (1, ALU.is_ge), (0, ALU.is_gt), (1, ALU.is_ge)]
            for i, (which, op) in enumerate(order):
                e.wait_ge(S["at_d"], i + 1)
                v = (AT, PT)[which][:, i // 2]
                e.affine_select(out=v, in_=v, compare_op=op, fill=0.0, base=0, pattern=[[0, GH], [1, P]],
                                channel_multiplier=-1).then_inc(S["at_p"], 1)
            e.wait_ge(S["at_d"], 5)
            e.affine_select(out=ATm[0:META], in_=ATm[0:META], compare_op=ALU.is_gt, fill=0.0, base=0,
                            pattern=[[0, GH], [1, META]], channel_multiplier=-1).then_inc(S["at_p"], 1)
            e.wait_ge(S["at_p"], 5)
            e.wait_ge(S["mask_in"], 16)
            for lv in range(7):
                for g in groups(lv):
                    if lv > 1:
                        e.wait_ge(S["x_mm"], count(lv - 1, g) + 1)
                    elif lv == 1:
                        e.wait_ge(S["t0_set"], g + 1)
                    if g < 2:
                        e.tensor_tensor(Al[:, g], AT[:, g], masks[:, lv, :].unsqueeze(1).broadcast_to([P, GH, P]),
                                        ALU.mult).then_inc(S["al_p"], 1)
                    else:
                        e.tensor_tensor(Alm[0:META], ATm[0:META], masks[0:META, lv, 0:META].unsqueeze(1)
                                        .broadcast_to([META, GH, META]), ALU.mult).then_inc(S["al_p"], 1)

        @block.scalar
        def _(e):
            e.wait_ge(S["cc_set"], 1)
            e.activation(ccol[:, 1, :], ccol[:, 4, :], ACT.Exp, scale=-1.0).then_inc(S["c_e"], 1)
            e.wait_ge(S["f_mm"], 1)
            e.activation(ftab[:, :], ps[0:HEADS, 6, 0:NDIST], ACT.Copy, scale=float(DH) ** 0.5).then_inc(S["f_sb"], 1)

            def split(t, slot, land, cols=False, words=SLOT, qs=range(4)):
                e.wait_ge(raw_in[slot], land)
                pw = words // 4
                for q in qs:
                    hb = q // 2
                    if q % 2 == 0:
                        halves_done = 2 * t + hb - 1
                        if not (isinstance(t, int) and halves_done <= 0):
                            e.wait_ge(S["split_used"], halves_done)
                    if cols:
                        src = raw[:, slot, 0:words].rearrange("p (k n) -> p k n", n=512)[
                            :, 4 * (q % 2):4 * (q % 2) + 4, 256 * hb:256 * hb + 256]
                        dst = wh[:, hb, 0:words // 2].rearrange("p (k n) -> p k n", n=256)[
                            :, 4 * (q % 2):4 * (q % 2) + 4, :]
                    else:
                        src = raw[:, slot, q * pw:(q + 1) * pw]
                        dst = wh[:, hb, (q % 2) * pw:(q % 2 + 1) * pw]
                    e.activation(dst, src, ACT.Copy).then_inc(S["split_h"], 1)

            nnorm = [0]
            nfm = [0]

            def stats(res, ready=None):
                for m in range(NM):
                    i = nnorm[0]
                    nnorm[0] += 1
                    if ready is not None:
                        e.wait_ge(*ready[m])
                    elif res:
                        e.wait_ge(S[("res_add", "res_add1")[m]], 2 * res)
                    else:
                        e.wait_ge(S["x_in"], 16)
                    e.activation(tok[:, m, :], x[:, m, :], ACT.Square, accum_out=stat[:, 0, m:m + 1]
                                 ).then_inc(S["sq_done"], 1)
                    e.wait_ge(S["sq_done"], i + 1)
                    e.activation(stat[:, 1, m:m + 1], stat[:, 0, m:m + 1], ACT.Sqrt, scale=1.0 / D, bias=epsc[:, :]
                                 ).then_inc(S["sc_chain"], 1)

            def to_hf(scale=None, shift=None):
                i = nfm[0]
                nfm[0] += 1
                for k in range(KD):
                    e.wait_ge(S["tr_done"], 4 * i + k // 2 + 1)
                    src = ps[:, 4 + k // 2, (k % 2) * SEQ:(k % 2 + 1) * SEQ]
                    if scale is None:
                        ins = e.activation(hf[:, k, META:TT], src, ACT.Copy)
                    elif shift is None:
                        ins = e.activation(hf[:, k, META:TT], src, ACT.Copy, scale=scale[:, k:k + 1])
                    else:
                        ins = e.activation(hf[:, k, META:TT], src, ACT.Identity,
                                           scale=scale[:, k:k + 1], bias=shift(k))
                    ins.then_inc(S["hf_done"], 1)

            def mlp_relu(it, t):
                for m in range(NM):
                    if m == 0:
                        e.wait_ge(S["u_done"], it + 1)
                    else:
                        e.wait_ge(S["split_used"], 2 * t + 2)
                    e.activation(relu[:, m, :], ps[:, 4 + m, :], ACT.Relu).then_inc(S["r_done"], 1)

            def mlp_aT(it):
                for b in range(2):
                    e.wait_ge(S["t_done"], 2 * it + b + 1)
                    e.activation(aTh[:, 2 * b:2 * b + 2, :],
                                 ps[:, 6 + b, :].rearrange("p (k t) -> p k t", k=2), ACT.Copy).then_inc(S["th_done"], 1)

            stats(0)
            e.wait_ge(S["mods_set"], 1)
            to_hf(mods[:, 0], lambda k: modc[:, 0, k:k + 1])
            split(T_POOL, *landed(N_POOL), words=HALF)
            for g in range(4):
                e.wait_ge(S["pool_chain"], 4 + g + 1)
                e.activation(H[:, 2 * g:2 * g + 2, META:TT], hf[:, 2 * g:2 * g + 2, META:TT], ACT.Copy
                             ).then_inc(S["hs_h"], 1)
            stats(1)
            split(T_MLP0, *landed(N_MLP0))
            e.wait_ge(S["mods_set"], 2)
            to_hf(mods[:, 1], lambda k: modc[:, 0, 24 + k:25 + k])

            split(T_MLP0 + 1, *landed(14), qs=(0, 1))
            mlp_relu(0, T_MLP0)
            split(T_MLP0 + 1, *landed(14), qs=(2, 3))
            mlp_aT(0)
            with e.Fori(1, 7) as j:
                split(T_MLP0 + 2 * j, 3, 16 * (3 + j))
                mlp_relu(j, T_MLP0 - 1 + 2 * j)
                split(T_MLP0 + 1 + 2 * j, 2, 16 * (4 + j))
                mlp_aT(j)
            split(T_MLP0 + 14, *landed(39))
            mlp_relu(7, T_MLP0 + 13)
            mlp_aT(7)
            split(T_MLP0 + 15, *landed(40))
            stats(2)
            split(T_QKV, *landed(N_QKV), cols=True, qs=(0, 1))
            e.wait_ge(S["mods_set"], 3)
            to_hf(mods[:, 2], lambda k: modc[:, 1, k:k + 1])
            split(T_QKV, *landed(N_QKV), cols=True, qs=(2, 3))
            for i in range(6):
                def next_half(hb):
                    split(T_QKV + i + 1, *landed(N_QKV + i + 1), cols=(i < 3), qs=(2 * hb, 2 * hb + 1))
                if i >= 4:
                    next_half(0)
                if i < 4:
                    e.wait_ge(S["split_used"], 2 * (T_QKV + i) + 1)
                else:
                    e.wait_ge(S["qkv_mm"], i - 3)
                b = 2 * (i % 4)
                if i < 4:
                    dst = (qT, kT)[i // 2][:, 4 * (i % 2):4 * (i % 2) + 2, :]
                    e.activation(dst, ps[:, b, :].rearrange("p (k t) -> p k t", k=2), ACT.Copy).then_inc(S["ev_act"], 1)
                else:
                    e.activation(v_tok[:, 0, 512 * (i - 4):512 * (i - 3)], ps[:, b, :], ACT.Copy).then_inc(S["ev_act"], 1)
                if i < 4:
                    next_half(0)
                next_half(1)
            for h in range(HEADS):
                for m in range(NM):
                    c0, w = ((256, 128), (0, 256))[m]
                    e.wait_ge(S["t_set"], 2 * h + m + 1)
                    if h >= 2 and m == 0:
                        e.wait_ge(S["pt_mm"], h - 1)
                    e.activation(P_sc[:, h % 2, c0:c0 + w], t_sc[:, h % 4, c0:c0 + w], ACT.Exp, scale=-1.0,
                                 bias=stat[:, 4 + m, h % 4:h % 4 + 1],
                                 accum_out=rsum[:, (h // 4) * 8 + m * 4 + h % 4:(h // 4) * 8 + m * 4 + h % 4 + 1]
                                 ).then_inc(S["p_set"], 1)
            e.wait_ge(S["mod_mm"], 19)
            to_hf()
            split(T_WO + 1, *landed(N_WO1))
            stats(3)
            split(T_MLP1, *landed(N_MLP1), qs=(0, 1))
            e.wait_ge(S["mods_set"], 4)
            to_hf(mods[:, 3], lambda k: modc[:, 1, 24 + k:25 + k])
            split(T_MLP1, *landed(N_MLP1), qs=(2, 3))
            split(T_MLP1 + 1, *landed(N_MLP1 + 1), qs=(0, 1))
            mlp_relu(8, T_MLP1)
            split(T_MLP1 + 1, *landed(N_MLP1 + 1), qs=(2, 3))
            mlp_aT(8)
            with e.Fori(0, 3) as i:
                for r in range(2):
                    n = N_MLP1 + 2 + 2 * r
                    split(T_MLP1 + 2 + 4 * i + 2 * r, n % R, 16 * (n // R + 1 + i))
                    mlp_relu(9 + 2 * i + r, T_MLP1 + 1 + 4 * i + 2 * r)
                    split(T_MLP1 + 3 + 4 * i + 2 * r, (n + 1) % R, 16 * ((n + 1) // R + 1 + i))
                    mlp_aT(9 + 2 * i + r)
            split(T_MLP1 + 14, *landed(N_MLP1 + 14))
            mlp_relu(15, T_MLP1 + 13)
            mlp_aT(15)
            split(T_MLP1 + 15, *landed(N_MLP1 + 15))
            e.wait_ge(S["xm_in"], 16)
            e.activation(tokm, xm, ACT.Square, accum_out=stat[0:META, 0, NM:NM + 1]).then_inc(S["sqm_done"], 1)
            e.wait_ge(S["sqm_done"], 1)
            e.activation(stat[0:META, 1, NM:NM + 1], stat[0:META, 0, NM:NM + 1], ACT.Sqrt, scale=1.0 / D,
                         bias=epsc[0:META, :]).then_inc(S["sqm_done"], 1)
            stats(4)
            stats(0, [(S["xp_done"], 1), (S["xp_done"], 2)])
            split(T_WIN, *landed(N_WIN), cols=True, qs=(0, 1))
            to_hf(pcol[:, 1, 16:24])
            split(T_WIN, *landed(N_WIN), cols=True, qs=(2, 3))
            for i in range(7):
                t = T_WIN + i

                def next_half(hb):
                    if i < 6:
                        split(t + 1, *landed(N_WIN + i + 1), cols=(i != 2), qs=(2 * hb, 2 * hb + 1))
                if i == 3:
                    next_half(0)
                    e.wait_ge(S["tk_d"], 3)
                    e.activation(tks[:, 2, :, :], tks[:, 1, :, :], ACT.Exp, scale=-1.0).then_inc(S["tk_a"], 1)
                    e.activation(eb[:, 0, :, :], sm[:, :, 0:4], ACT.Exp, scale=-1.0).then_inc(S["tk_a"], 1)
                    e.wait_ge(S["par2_in"], 64)
                    e.activation(nega[:, 0, :], alog[:, :], ACT.Exp).then_inc(S["tk_a"], 1)
                    e.wait_ge(S["tk_a"], 1)
                    e.activation(tks[:, 3, :, :], tks[:, 2, :, :], ACT.Ln, bias=ones[:, 0:1]).then_inc(S["tk_a"], 1)
                    for m in range(NM):
                        e.wait_ge(*((S["pj_mm"], 7) if m == 0 else (S["split_used"], 2 * t + 2)))
                        e.activation(zs[:, m, :], ps[:, m, :], ACT.Copy).then_inc(S["pj_ev"], 1)
                    next_half(1)
                    continue
                b = 4 if i % 2 == 0 else 0
                pj = (0, 2, 4, None, 7, 9, 11)[i]
                for c in range(4):
                    e.wait_ge(*((S["pj_mm"], pj + c // 2 + 1) if c % 2 == 0 else (S["split_used"], 2 * t + c // 2 + 1)))
                    if i == 0 and c == 0:
                        e.wait_ge(S["made2"], 7)
                    if i < 3:
                        blk = 4 * i + c
                        e.activation(gT[:, blk, 3:3 + TT], ps[:, b + c, 0:TT], ACT.Copy).then_inc(S["cv_ev"], 1)
                        e.activation(yT[:, blk, :], ps[:, b + c, 0:TT], ACT.Copy,
                                     scale=pcol[:, 1, 32 + 36 + blk:33 + 36 + blk]).then_inc(S["pj_ev"], 1)
                    else:
                        e.activation(fT[:, 4 * (i - 4) + c, :], ps[:, b + c, 0:TT], ACT.Copy).then_inc(S["pj_ev"], 1)
                    if c % 2:
                        next_half(c // 2)

            e.wait_ge(S["nc_mm"], 1)
            e.activation(ncT, ps[0:FH, 0, 0:TT], ACT.Copy, scale=float(DH) ** 0.5).then_inc(S["nc_set"], 1)
            e.wait_ge(S["gs_mm"], 1)
            e.activation(EG[:, 1:3, :], ps[:, 1, 0:24].rearrange("p (s c) -> p s c", s=2), ACT.Exp).then_inc(S["gs_set"], 1)
            e.wait_ge(S["gs_mm"], 2)
            e.activation(EG[0:META, 0, 4:8], ps[0:META, 2, 0:4], ACT.Exp).then_inc(S["gs_set"], 1)
            for i in range(3):
                e.wait_ge(S["conv"], 12 * i + 12)
                e.activation(yT[:, 4 * i:4 * i + 4, :], yT[:, 4 * i:4 * i + 4, :], ACT.Silu).then_inc(S["silu_set"], 1)
            e.activation(zs[:, :, :], zs[:, :, :], ACT.Silu).then_inc(S["silu_set"], 1)
            for h in range(FH + 1):
                if h < FH:
                    for m in range(NM):
                        c0, w = ((TT, META + P), (0, TT))[m]
                        e.wait_ge(S["ft_set"], 2 * h + m + 1)
                        if h >= 2 and m == 0:
                            e.wait_ge(S["fpt_mm"], h - 1)
                        e.activation(P_f[:, h % 2, c0:c0 + w], t_f[:, h % 2, c0:c0 + w], ACT.Exp, scale=-1.0,
                                     bias=stat[:, 4 + m, h % 2:h % 2 + 1],
                                     accum_out=rf[:, FH * m + h:FH * m + h + 1]).then_inc(S["fp_set"], 1)
                if h == 0:
                    e.wait_ge(S["vt_mm"], 3)
                    e.activation(vtm, ps[0:META, 2, :], ACT.Copy).then_inc(S["vtm_ev"], 1)
                if h >= 1:
                    e.wait_ge(S["fpt_mm"], h)
                    if h >= 3:
                        e.wait_ge(S["fo_mm"], h - 2)
                    e.activation(PTb[:, (h - 1) % 2, :], ps[0:META, 6 + (h - 1) % 2, 0:256], ACT.Copy
                                 ).then_inc(S["fpb_ev"], 1)
            for i, (dst, src) in enumerate([(v_t[:, 0], ps[:, 4, :]), (v_t[:, 1], ps[:, 5, :]),
                                            (kv_m[:, 0], ps[0:META, 6, :]), (kv_m[:, 1], ps[0:META, 7, :])]):
                e.wait_ge(S["gt_mm"], 5 + i)
                e.activation(dst, src.rearrange("p (h d) -> p h d", h=GH), ACT.Copy).then_inc(S["gt_a"], 1)
            for m in range(NM):
                e.wait_ge(S["gt_d"], m + 1)
                for h in range(GH):
                    e.activation(junk[:, 4 * m + h, :], q_t[:, m, h, :], ACT.Square,
                                 accum_out=nrm[:, 0, 0, 1 + m, h:h + 1]).then_inc(S["nrm_sq"], 1)
            e.wait_ge(S["nrm_sq"], NM * GH)
            e.wait_ge(S["nk_sq"], 6)
            e.activation(nrm[:, 1, 0], nrm[:, 0, 0], ACT.Sqrt, scale=float(P), bias=epsq[:, :]).then_inc(S["nrm_sq"], 1)
            e.activation(nrm[:, 1, 1], nrm[:, 0, 1], ACT.Sqrt, bias=epsc[:, :]).then_inc(S["nrm_sq"], 1)
            for g in range(3):
                e.wait_ge(S["d_mm"], g + 1)
                if g < 2:
                    e.activation(E_[:, g], ps[:, 6 + g, :].rearrange("p (h c) -> p h c", h=GH), ACT.Exp).then_inc(S["e_set"], 1)
                else:
                    e.activation(Em[0:META], ps[0:META, 5, 0:64].rearrange("p (h c) -> p h c", h=GH), ACT.Exp
                                 ).then_inc(S["e_set"], 1)
            def hv(b, n=P, w=P):
                return ps[0:n, b, 0:GH * w].rearrange("p (h c) -> p h c", h=GH)
            for m in range(NM):
                e.wait_ge(S["tt_mm"], 5 * m + 2)
                e.activation(KbT[:, m], hv(1), ACT.Copy).then_inc(S["tt_a"], 1)
                e.wait_ge(S["tt_mm"], 5 * m + 4)
                e.activation(QgT[:, m], hv(3), ACT.Copy).then_inc(S["tt_a"], 1)
            for g in range(3):
                e.wait_ge(S["t0_mm"], g + 1)
                if g < 2:
                    e.activation(T_[:, g], hv(g), ACT.Copy).then_inc(S["t0_ev"], 1)
                else:
                    e.activation(Tm[0:META], hv(2, META, META), ACT.Copy).then_inc(S["t0_ev"], 1)
            for lv in range(1, 7):
                for g in groups(lv):
                    e.wait_ge(S["x_mm"], count(lv, g) + 1)
                    if g < 2:
                        e.activation(X[:, g], hv(g), ACT.Copy).then_inc(S["x_ev"], 1)
                    else:
                        e.activation(Xm[0:META], hv(2, META, META), ACT.Copy).then_inc(S["x_ev"], 1)
            for i, (dst, src) in enumerate([(um[:, :, :], hv(4, META)), (u[:, 0], hv(0)), (u[:, 1], hv(1))]):
                e.wait_ge(S["uw_mm"], i + 1)
                e.activation(dst, src, ACT.Copy).then_inc(S["u_ev"], 1)
            for m in range(NM):
                e.wait_ge(S["go_mm"], m + 1)
                for h in range(GH):
                    e.activation(junk_o[:, 4 * m + h, :], ps[:, m, P * h:P * h + P], ACT.Square,
                                 accum_out=onrm[:, 0, m, h:h + 1]).then_inc(S["on_sq"], 1)
                e.wait_ge(S["on_sq"], 5 * m + 4)
                e.activation(onrm[:, 1, m, :], onrm[:, 0, m, :], ACT.Sqrt, scale=1.0 / P, bias=epsc[:, :]
                             ).then_inc(S["on_sq"], 1)
                if m == 0:
                    e.wait_ge(S["s1_mm"], 1)
                    split(T_WOUT, *landed(N_WOUT))
            to_hf()
            split(T_WOUT + 1, *landed(N_WOUT + 1))
            stats(0, [(S["r2_add"], 2), (S["r2_add"], 4)])
            split(T_FFN, N_FFN % R, before(N_FFN) + 32, qs=(0, 1))
            to_hf(pcol[:, 1, 24:32])
            split(T_FFN, N_FFN % R, before(N_FFN) + 32, qs=(2, 3))

            def g_silu(j, t):
                for m in range(NM):
                    e.wait_ge(*((S["gu_done"], j + 1) if m == 0 else (S["split_used"], 2 * t + 2)))
                    e.activation(relu[:, m, 0:256], ps[:, 4 + m, 0:256], ACT.Silu).then_inc(S["gr_done"], 1)

            def g_aT(j):
                e.wait_ge(S["gt_done"], j + 1)
                e.activation(aTh[:, 0:2, :], ps[:, 6, :].rearrange("p (k t) -> p k t", k=2), ACT.Copy).then_inc(S["gth_done"], 1)

            def g_slot(n, i=0):
                seen = sum(2 if (k - N_FFN == 0 or (k - N_FFN) % 2 == 1) and k != N_FFN + 21 else 1
                           for k in range(N_FFN, n + 1) if k % R == n % R)
                step = 32 if (n - N_FFN) % 2 == 1 else 16
                return n % R, before(n) + 16 * seen + step * i
            split(T_FFN + 1, *g_slot(N_FFN + 1), qs=(0, 1))
            g_silu(0, T_FFN)
            split(T_FFN + 1, *g_slot(N_FFN + 1), qs=(2, 3))
            g_aT(0)

            def g_body(i, last=False):
                for r in range(2):
                    split(T_FFN + 2 + 2 * r + 4 * i, *g_slot(N_FFN + 2 + 2 * r, i), words=HALF)
                    g_silu(1 + r + 2 * i, T_FFN + 1 + 2 * r + 4 * i)
                    if not (last and r):
                        split(T_FFN + 3 + 2 * r + 4 * i, *g_slot(N_FFN + 3 + 2 * r, i))
                    g_aT(1 + r + 2 * i)
            with e.Fori(0, 4) as i:
                g_body(i)
            g_body(4, last=True)
            split(T_FFN + 21, *g_slot(N_FFN + 21), words=HALF)
            stats(0, [(S["r2_add"], 6), (S["r2_add"], 8)])

        @block.vector
        def _(e):
            e.wait_ge(S["ptr"], 1)
            e.tensor_copy(ccol[:, 4, :], ps[:, 7, 256:264]).then_inc(S["cc_set"], 1)
            e.wait_ge(S["c_e"], 1)
            e.tensor_scalar(ccol[:, 2, :], ccol[:, 1, :], 1.0, None, ALU.add).then_inc(S["c_s"], 1)
            e.wait_ge(S["c_s"], 1)
            e.reciprocal(ccol[:, 3, :], ccol[:, 2, :]).then_inc(S["c_s"], 1)
            e.wait_ge(S["c_s"], 2)
            e.tensor_tensor(ccol[:, 0, :], ccol[:, 3, :], ccol[:, 4, :], ALU.mult).then_inc(S["c_s"], 1)
            e.wait_ge(S["c_s"], 3)
            nch = [0]

            def mod_sum(u):
                n = MOD0_LOADS[u]
                e.wait_ge(raw_in[n % R], landed(n)[1])
                if u >= 2:
                    e.wait_ge(S["mod_mm"], u - 1)
                w, dst = kview(n % R), acc[:, u % 2, :]
                for k in range(MOD0_PE[u], KD):
                    if k == MOD0_PE[u]:
                        ins = e.tensor_scalar(dst, w[:, k, :], ccol[:, 0, k:k + 1], None, ALU.mult)
                    else:
                        e.wait_ge(S["mod_chain"], nch[0])
                        ins = e.scalar_tensor_tensor(out=dst, in0=w[:, k, :], scalar=ccol[:, 0, k:k + 1],
                                                     in1=dst, op0=ALU.mult, op1=ALU.add)
                    if k < KD - 1:
                        nch[0] += 1
                        ins.then_inc(S["mod_chain"], 1)
                    else:
                        ins.then_inc(S["mod_acc" if u < 11 else "mod_accb"], 1)

            def mod_cols(u):
                e.wait_ge(S["mod_mm"], u + 1)
                e.tensor_tensor(modc[:, 0, 4 * u:4 * u + 4], ps[:, 2, 0:4], pcol[:, 0, 4 * u:4 * u + 4], ALU.add
                                ).then_inc(S["mod_col"], 1)

            def mod_halves(j):
                base = nch[0] + 14 * (j - 2)
                for k in range(KD):
                    for hb in range(2):
                        w, dst = kview(hb), acc[:, hb, 0:256]
                        if k == 0:
                            e.wait_ge(raw_in[hb], 16 * (j + 3))
                            if hb == 0:
                                e.wait_ge(S["mod_mm"], 10 + j)
                            ins = e.tensor_scalar(dst, w[:, 0, 0:256], ccol[:, 0, 0:1], None, ALU.mult)
                        else:
                            e.wait_ge(S["mod_chain"], base + 2 * k - 1 + hb)
                            ins = e.scalar_tensor_tensor(out=dst, in0=w[:, k, 0:256], scalar=ccol[:, 0, k:k + 1],
                                                         in1=dst, op0=ALU.mult, op1=ALU.add)
                        ins.then_inc(S["mod_chain"] if k < KD - 1 else S[("mod_acc", "mod_accb")[hb]], 1)

            def mod_unit(u, ks):
                w = raw[:, (N_MOD1 + u) % R, 0:KD * MUW].rearrange("p (k n) -> p k n", k=KD)
                for k in ks:
                    if k == 0:
                        e.wait_ge(raw_in[(N_MOD1 + u) % R], landed(N_MOD1 + u)[1])
                        ins = e.tensor_scalar(accu[:, u, :], w[:, 0, :], ccol[:, 0, 0:1], None, ALU.mult)
                    else:
                        e.wait_ge(S["mod_chain"], nch[0])
                        ins = e.scalar_tensor_tensor(out=accu[:, u, :], in0=w[:, k, :], scalar=ccol[:, 0, k:k + 1],
                                                     in1=accu[:, u, :], op0=ALU.mult, op1=ALU.add)
                    if k < KD - 1:
                        nch[0] += 1
                        ins.then_inc(S["mod_chain"], 1)
                    else:
                        ins.then_inc(S["mod_accu"], 1)

            def mod_cols1(j):
                e.wait_ge(S["mod_mm"], 11 + j)
                if isinstance(j, int):
                    dst, b = modc[:, 1, 4 * j - 8:4 * j - 4], pcol[:, 0, 48 + 4 * j - 8:48 + 4 * j - 4]
                else:
                    dst, b = modc[:, 1, bass.ds(4 * j - 8, 4)], pcol[:, 0, bass.ds(48 + 4 * j - 8, 4)]
                e.tensor_tensor(dst, ps[:, 5, 0:4], b, ALU.add).then_inc(S["mod_col"], 1)

            mod_sum(0)
            e.wait_ge(S["ptr"], 2)
            e.tensor_copy(pcol[:, 0, :], ps[:, 7, 0:P]).then_inc(S["pcopied"], 1)
            e.tensor_copy(pcol[:, 1, 0:80], ps[:, 7, P:P + 80]).then_inc(S["pcopied"], 1)
            e.wait_ge(S["made"], 7)
            e.reciprocal(inv16[:, :], inv16[:, :]).then_inc(S["c_s"], 1)
            Z0 = META - 8
            for w in range(2):
                e.memset(win[w][:, :, Z0:META], 0.0).then_inc(S["c_s"], 1)
            e.memset(hf[:, :, Z0:META], 0.0).then_inc(S["c_s"], 1)
            e.wait_ge(S["c_s"], 7)
            e.wait_ge(S["pcopied"], 2)
            mod_sum(1)
            mod_cols(0)

            def scale_cols(i, l, w, sec):
                e.scalar_tensor_tensor(out=mods[:, i, :], in0=modc[:, l, 8 * sec:8 * sec + 8], scalar=1.0,
                                       in1=pcol[:, 0, w:w + 8], op0=ALU.add, op1=ALU.mult).then_inc(S["mods_set"], 1)

            ngate = [0]

            def gate_diag(col):
                for k in range(KD):
                    e.tensor_scalar(diag[:, k, :], ident[:, :], col[:, k:k + 1], None, ALU.mult).then_inc(S["gate_diag"], 1)

            def gate_copy(dst, b=0):
                i = ngate[0]
                ngate[0] += 1
                for c in range(2):
                    e.wait_ge(S["gate_mm"], 2 * i + c + 1)
                    e.tensor_copy(gate[dst][:, 512 * c:512 * c + 512], ps[:, b + c, :]).then_inc(S["gate_set"], 1)

            nn = [0]

            def rstd(m):
                i = nn[0]
                nn[0] += 1
                e.wait_ge(S["sc_chain"], i + 1)
                e.reciprocal(stat[:, 2, m:m + 1], stat[:, 1, m:m + 1]).then_inc(S["rstd_done"], 1)
                e.wait_ge(S["rstd_done"], i + 1)

            def normalise_tile(m):
                rstd(m)
                e.tensor_scalar(tok[:, m, :], x[:, m, :], stat[:, 2, m:m + 1], None, ALU.mult).then_inc(S["xn_done"], 1)

            def normalise():
                for m in range(NM):
                    normalise_tile(m)

            nhf = [0]

            def split_h(c0=META):
                i = nhf[0]
                nhf[0] += 1
                for b in range(4):
                    e.wait_ge(S["hf_done"], 8 * i + 2 * b + 2)
                    s = slice(2 * b, 2 * b + 2)
                    e.tensor_copy(H[:, s, c0:TT], hf[:, s, c0:TT]).then_inc(S["hs_h"], 1)
                    e.wait_ge(S["hs_h"], 4 * i + b + 1)
                    e.tensor_tensor(L[:, s, c0:TT], hf[:, s, c0:TT], H[:, s, c0:TT].bitcast(F32), ALU.subtract
                                    ).then_inc(S["hs_l"], 1)

            def split(t, slot, cols=False, words=SLOT, qs=range(4)):
                pw = words // 4
                for q in qs:
                    e.wait_ge(S["split_h"], 4 * t + q + 1)
                    hb = q // 2
                    if cols:
                        src = raw[:, slot, 0:words].rearrange("p (k n) -> p k n", n=512)[
                            :, 4 * (q % 2):4 * (q % 2) + 4, 256 * hb:256 * hb + 256]
                        o, i1 = (w[:, hb, 0:words // 2].rearrange("p (k n) -> p k n", n=256)[
                            :, 4 * (q % 2):4 * (q % 2) + 4, :] for w in (wl, wh))
                    else:
                        src = raw[:, slot, q * pw:(q + 1) * pw]
                        o, i1 = (w[:, hb, (q % 2) * pw:(q % 2 + 1) * pw] for w in (wl, wh))
                    e.tensor_tensor(o, src, i1.bitcast(F32), ALU.subtract).then_inc(S["split_l"], 1)

            nr = [0]

            def residual(g, gs, done, b=0, then=None):
                i = nr[0]
                nr[0] += 1
                e.wait_ge(S["gate_set"], gs)

                def gated(m, c):
                    e.wait_ge(*done[2 * m + c])
                    e.tensor_tensor(tok[:, m, 512 * c:512 * c + 512], ps[:, b + 2 * m + c, :],
                                    gate[g][:, 512 * c:512 * c + 512], ALU.mult).then_inc(S["res_mul"], 1)

                def add(c):
                    e.wait_ge(S["res_mul"], 4 * i + 3 + c)
                    e.tensor_tensor(x[:, 1, 512 * c:512 * c + 512], x[:, 1, 512 * c:512 * c + 512],
                                    tok[:, 1, 512 * c:512 * c + 512], ALU.add).then_inc(S["res_add1"], 1)
                gated(0, 0)
                gated(0, 1)
                gated(1, 0)
                add(0)
                if then is not None:
                    then(0)
                gated(1, 1)
                add(1)
                if then is not None:
                    then(1)

            def mlp_aT(it):
                for b in range(2):
                    e.wait_ge(S["th_done"], 2 * it + b + 1)
                    e.tensor_tensor(aTl[:, 2 * b:2 * b + 2, :], ps[:, 6 + b, :].rearrange("p (k t) -> p k t", k=2),
                                    aTh[:, 2 * b:2 * b + 2, :].bitcast(F32), ALU.subtract).then_inc(S["tl_done"], 1)

            normalise()
            mod_sum(2)
            mod_cols(1)
            mod_sum(3)
            mod_cols(2)
            mod_cols(3)
            e.wait_ge(S["mod_col"], 4)
            scale_cols(0, 0, 96, 1)
            nhf[0] = 1
            e.wait_ge(S["hf_done"], 8)
            src = hf
            for lv in range(4):
                dst = win[lv % 2]
                if lv:
                    e.wait_ge(S["pool_chain"], lv)
                k0 = 2 * lv
                e.tensor_tensor(dst[:, k0:, META:TT], src[:, k0:, META:TT], src[:, k0:, META - 2 ** lv:TT - 2 ** lv],
                                ALU.add).then_inc(S["pool_chain"], 1)
                src = dst
            split(T_POOL, landed(N_POOL)[0], words=HALF)
            mod_sum(4)
            e.wait_ge(S["pool_chain"], 4)
            pooled = hf
            for g in range(4):
                w = 2 ** (g + 1)
                sums, ks = win[g % 2], slice(2 * g, 2 * g + 2)
                e.tensor_tensor(sums[:, ks, META:META + w], sums[:, ks, META:META + w],
                                inv16[:, 0:w].unsqueeze(1).broadcast_to([P, 2, w]), ALU.mult).then_inc(S["c_s"], 1)
                e.wait_ge(S["c_s"], 7 + 2 * g + 1)
                e.tensor_tensor(pooled[:, ks, META:META + w], sums[:, ks, META:META + w],
                                hf[:, ks, META:META + w], ALU.subtract).then_inc(S["c_s"], 1)
                e.scalar_tensor_tensor(out=pooled[:, ks, META + w:TT], in0=sums[:, ks, META + w:TT], scalar=1.0 / w,
                                       in1=hf[:, ks, META + w:TT], op0=ALU.mult, op1=ALU.subtract
                                       ).then_inc(S["pool_chain"], 1)
                e.wait_ge(S["hs_h"], g + 1)
                e.tensor_tensor(L[:, ks, META:TT], hf[:, ks, META:TT], H[:, ks, META:TT].bitcast(F32), ALU.subtract
                                ).then_inc(S["hs_l"], 1)
                if g == 1:
                    mod_cols(4)
                    mod_sum(5)
            mod_cols(5)
            e.wait_ge(S["mod_col"], 6)
            e.tensor_tensor(mods[:, 4, :], modc[:, 0, 16:24], pcol[:, 1, 8:16], ALU.mult).then_inc(S["pg_set"], 1)
            e.wait_ge(S["pg_set"], 1)
            gate_diag(mods[:, 4, :])
            mod_sum(6)
            gate_copy(0)
            used, y = S["split_used"], S["y_done"]
            residual(0, 2, [(y, 1), (y, 2), (used, 2 * T_POOL + 1), (used, 2 * T_POOL + 2)], b=4)
            mod_cols(6)
            mod_sum(7)
            mod_sum(8)
            mod_cols(7)
            normalise()
            mod_sum(9)
            mod_cols(8)
            split(T_MLP0, landed(N_MLP0)[0])
            mod_cols(9)
            e.wait_ge(S["mod_col"], 10)
            scale_cols(1, 0, 112, 4)
            split_h()
            mod_sum(10)
            split(T_MLP0 + 1, landed(14)[0], qs=(0, 1))
            mod_sum(11)
            split(T_MLP0 + 1, landed(14)[0], qs=(2, 3))
            mlp_aT(0)
            split(T_MLP0 + 2, 3)
            split(T_MLP0 + 3, 2)
            e.wait_ge(S["mod_mm"], 12)
            e.tensor_tensor(modc[:, 0, 40:48], ps[:, 5, 0:8], pcol[:, 0, 40:48], ALU.add).then_inc(S["mod_col"], 2)
            mlp_aT(1)
            with e.Fori(2, 7) as j:
                split(T_MLP0 + 2 * j, 3)
                mod_halves(j)
                split(T_MLP0 + 1 + 2 * j, 2)
                mod_cols1(j)
                mlp_aT(j)
            mod_halves(7)
            nch[0] += 14 * 6
            split(T_MLP0 + 14, 3)
            gate_diag(modc[:, 0, 40:48])
            mod_cols1(7)
            mlp_aT(7)
            split(T_MLP0 + 15, 0)
            gate_copy(1, 4)
            e.wait_ge(S["mod_col"], 18)
            scale_cols(2, 1, 104, 1)
            residual(1, 4, [(y, 3), (y, 4), (y, 5), (used, 2 * (T_MLP0 + 16))], then=normalise_tile)
            split(T_QKV, landed(N_QKV)[0], cols=True, qs=(0, 1))
            split_h()
            split(T_QKV, landed(N_QKV)[0], cols=True, qs=(2, 3))
            for i in range(6):
                split(T_QKV + i + 1, landed(N_QKV + i + 1)[0], cols=(i < 3), qs=(0, 1))
                e.wait_ge(S["split_used"], 2 * (T_QKV + i) + 2)
                b = 2 * (i % 4) + 1
                if i < 4:
                    dst = (qT, kT)[i // 2][:, 4 * (i % 2) + 2:4 * (i % 2) + 4, :]
                    e.tensor_copy(dst, ps[:, b, :].rearrange("p (k t) -> p k t", k=2)).then_inc(S["ev_dve"], 1)
                else:
                    e.tensor_copy(v_tok[:, 1, 512 * (i - 4):512 * (i - 3)], ps[:, b, :]).then_inc(S["ev_dve"], 1)
                split(T_QKV + i + 1, landed(N_QKV + i + 1)[0], cols=(i < 3), qs=(2, 3))
            e.wait_ge(S["tb_in"], 16)

            def backwards(v):
                (s0, n0), (s1, n1) = v.ap
                return bass.AP(tensor=v.tensor, offset=v.offset + s1 * (n1 - 1), ap=[[s0, n0], [-s1, n1]])

            def scores(h):
                for m in range(NM):
                    c0, w = ((256, 128), (0, 256))[m]
                    e.wait_ge(S["s_mm"], h + 1)
                    if h >= 4:
                        e.wait_ge(S["p_set"], 2 * (h - 4) + m + 1)
                    e.tensor_tensor_reduce(out=t_sc[:, h % 4, c0:c0 + w], in0=ps[:, 4 + h % 4, c0:c0 + w],
                                           in1=backwards(TB[:, h, 0:w]), scale=-float(DH) ** -0.5, scalar=3e38,
                                           op0=ALU.add, op1=ALU.min,
                                           accum_out=stat[:, 4 + m, h % 4:h % 4 + 1]).then_inc(S["t_set"], 1)

            def evac(h):
                e.wait_ge(S["pt_mm"], h + 1)
                if h >= 2:
                    e.wait_ge(S["o_mm"], h - 1)
                e.tensor_copy(PT_sc[:, h % 2, :], ps[:, 2 + h % 2, 0:384]).then_inc(S["pt_ev"], 1)

            def norm_o(g):
                e.wait_ge(S["p_set"], 8 * g + 8)
                e.reciprocal(rrec[:, 8 * g:8 * g + 8], rsum[:, 8 * g:8 * g + 8]).then_inc(S["rec_set"], 1)
                e.wait_ge(S["rec_set"], g + 1)
                e.wait_ge(S["o_mm"], 4 * g + 4)
                e.tensor_tensor(tok[:, :, 256 * g:256 * g + 256].rearrange("p m (h d) -> p m h d", h=4),
                                ps[:, g % 2, :].rearrange("p (m h d) -> p m h d", m=2, h=4),
                                rrec[:, 8 * g:8 * g + 8].rearrange("p (m h) -> p m h", m=2).unsqueeze(3)
                                .broadcast_to([P, 2, 4, DH]), ALU.mult).then_inc(S["o_ev"], 1)
            e.wait_ge(S["split_used"], 2 * T_WO)
            for h in range(HEADS + 3):
                if 2 <= h < HEADS + 2:
                    evac(h - 2)
                if h < HEADS:
                    scores(h)
                    mod_unit(h // 2, range(4 * (h % 2), 4 * (h % 2) + 4))
                if h >= 6 and (h - 6) % 4 == 0:
                    norm_o((h - 6) // 4)
            e.wait_ge(S["mod_mm"], 19)
            e.tensor_tensor(modc[:, 1, 24:48], ps[:, 4, 0:24], pcol[:, 0, 72:96], ALU.add).then_inc(S["mod_col"], 1)
            e.wait_ge(S["mod_col"], 19)
            scale_cols(3, 1, 120, 4)
            e.wait_ge(S["s_mm"], HEADS)
            e.wait_ge(S["o_ev"], 4)
            gate_diag(modc[:, 1, 16:24])
            gate_copy(0)
            gate_diag(modc[:, 1, 40:48])
            gate_copy(1)
            split_h()
            split(T_WO + 1, landed(N_WO + 1)[0])
            residual(0, 6, [(y, 6), (y, 7), (used, 2 * T_WO + 2), (used, 2 * T_WO + 4)], then=normalise_tile)
            split(T_MLP1, landed(N_MLP1)[0], qs=(0, 1))
            split_h()
            split(T_MLP1, landed(N_MLP1)[0], qs=(2, 3))
            split(T_MLP1 + 1, landed(N_MLP1 + 1)[0])
            mlp_aT(8)
            with e.Fori(0, 3) as i:
                for r in range(2):
                    n = N_MLP1 + 2 + 2 * r
                    split(T_MLP1 + 2 + 4 * i + 2 * r, n % R)
                    split(T_MLP1 + 3 + 4 * i + 2 * r, (n + 1) % R)
                    mlp_aT(9 + 2 * i + r)
            split(T_MLP1 + 14, 3)
            mlp_aT(15)
            split(T_MLP1 + 15, 0)
            def first_output(m):
                if m == 0:
                    e.wait_ge(S["row_in"], 16)
                rstd(m)
                e.scalar_tensor_tensor(out=x[:, m, :], in0=x[:, m, :], scalar=stat[:, 2, m:m + 1], in1=gate[0][:, :],
                                       op0=ALU.mult, op1=ALU.mult).then_inc(S["xp_done"], 1)
            e.wait_ge(S["sqm_done"], 2)
            e.reciprocal(stat[0:META, 2, NM:NM + 1], stat[0:META, 1, NM:NM + 1]).then_inc(S["sqm_done"], 1)
            residual(1, 8, [(y, 8), (y, 9), (y, 10), (used, 2 * (T_MLP1 + 16))], then=first_output)
            normalise()
            split(T_WIN, landed(N_WIN)[0], cols=True, qs=(0, 1))
            e.wait_ge(S["sqm_done"], 3)
            e.tensor_scalar(tokm, xm, stat[0:META, 2, NM:NM + 1], None, ALU.mult).then_inc(S["xnm_done"], 1)
            e.wait_ge(S["mtr_done"], 1)
            e.tensor_tensor(hf[:, :, 0:META], ps[:, 3, 0:KD * META].rearrange("p (k t) -> p k t", k=KD),
                            pcol[:, 1, 16:24].unsqueeze(2).broadcast_to([P, KD, META]), ALU.mult).then_inc(S["hfm_done"], 1)
            e.wait_ge(S["hfm_done"], 1)
            split_h(0)
            split(T_WIN, landed(N_WIN)[0], cols=True, qs=(2, 3))
            e.wait_ge(S["sm_mm"], 1)
            e.wait_ge(S["made2"], 6)
            e.tensor_copy(sm[0:META, 0, :], ps[0:META, 3, 256:272]).then_inc(S["sm_set"], 1)
            e.tensor_copy(sm[:, 1:3, :], ps[:, 3, 272:304].rearrange("p (s c) -> p s c", s=2)).then_inc(S["sm_set"], 1)

            def conv(i):
                for j in (2, 1, 0):
                    for c in range(4):
                        blk = 4 * i + c
                        if j == 2:
                            e.wait_ge(S["pj_ev"], blk + 1)
                        else:
                            e.wait_ge(S["conv"], 12 * i + 4 * (1 - j) + c + 1)
                        e.scalar_tensor_tensor(out=yT[:, blk, :], in0=gT[:, blk, j:j + TT],
                                               scalar=pcol[:, 1, 32 + 12 * j + blk:33 + 12 * j + blk],
                                               in1=yT[:, blk, :], op0=ALU.mult, op1=ALU.add).then_inc(S["conv"], 1)
            for i in range(1, 7):
                split(T_WIN + i, landed(N_WIN + i)[0], cols=(i != 3))
                if i <= 3:
                    conv(i - 1)
                if i == 2:
                    e.wait_ge(S["sm_set"], 2)
                    e.wait_ge(S["par2_in"], 64)
                    e.tensor_tensor(tks[:, 0, :, 0:4], sm[:, :, 4:8], dtb[:, :].unsqueeze(1).broadcast_to([P, 3, 4]),
                                    ALU.add).then_inc(S["tk_d"], 1)
                    e.scalar_tensor_tensor(out=tks[:, 0, :, 4:12], in0=sm[:, :, 8:16], scalar=-1.0,
                                           in1=fgb[:, :].unsqueeze(1).broadcast_to([P, 3, 8]),
                                           op0=ALU.mult, op1=ALU.subtract).then_inc(S["tk_d"], 1)
                    e.wait_ge(S["tk_d"], 2)
                    e.scalar_tensor_tensor(out=tks[:, 1, :, :], in0=tks[:, 0, :, :], scalar=-1.0, in1=tks[:, 0, :, :],
                                           op0=ALU.mult, op1=ALU.max).then_inc(S["tk_d"], 1)
                if i == 4:
                    e.wait_ge(S["tk_a"], 2)
                    e.tensor_scalar(eb[:, 1], eb[:, 0], 1.0, None, ALU.add).then_inc(S["tk_d"], 1)
                    e.wait_ge(S["tk_d"], 4)
                    e.reciprocal(beta[:, :, :], eb[:, 1]).then_inc(S["tk_d"], 1)
                    e.wait_ge(S["tk_a"], 3)
                    e.tensor_scalar(nega[:, 1, :], nega[:, 0, :], -1.0, None, ALU.mult).then_inc(S["tk_d"], 1)
                    e.wait_ge(S["tk_a"], 4)
                    e.scalar_tensor_tensor(out=tks[:, 1], in0=tks[:, 0], scalar=0.0, in1=tks[:, 3],
                                           op0=ALU.max, op1=ALU.add).then_inc(S["tk_d"], 1)
                    e.wait_ge(S["tk_d"], 7)
                    e.tensor_tensor(gdec[:, :, :], tks[:, 1, :, 0:4], nega[:, 1, :].unsqueeze(1).broadcast_to([P, 3, 4]),
                                    ALU.mult).then_inc(S["tk_d"], 1)
            for h in range(FH):
                e.wait_ge(S["bc_mm"], h + 1)
                e.tensor_copy(cm1[:, h, :], ps[:, (3, 0)[h % 2], 0:TT]).then_inc(S["cm_raw"], 1)
            for h in range(FH + 2):
                g = h - 2
                if g >= 0:
                    e.wait_ge(S["fpt_mm"], g + 1)
                    if g >= 2:
                        e.wait_ge(S["fo_mm"], g - 1)
                    e.tensor_copy(PTa[:, g % 2, :], ps[:, 2 + g % 2, 0:384]).then_inc(S["fpa_ev"], 1)
                if h < FH:
                    e.wait_ge(S["fs_mm"], h + 1)
                    e.wait_ge(S["cm_set"], 2 if h < 4 else 4)
                    for m in range(NM):
                        c0, w = ((TT, META + P), (0, TT))[m]
                        if h >= 2:
                            e.wait_ge(S["fp_set"], 2 * (h - 2) + m + 1)
                        e.tensor_tensor_reduce(out=t_f[:, h % 2, c0:c0 + w], in0=ps[:, 4 + h % 2, c0:c0 + w],
                                               in1=(cm0, cm1)[m][:, h, :], scale=-float(DH) ** -0.5, scalar=3e38,
                                               op0=ALU.add, op1=ALU.min,
                                               accum_out=stat[:, 4 + m, h % 2:h % 2 + 1]).then_inc(S["ft_set"], 1)
                if h == 0:
                    for m in range(NM):
                        e.wait_ge(S["vt_mm"], m + 1)
                        e.tensor_copy(vt[:, m, :], ps[:, 6 + m, :]).then_inc(S["vt_ev"], 1)
            e.wait_ge(S["fp_set"], 2 * FH)
            e.reciprocal(rrec[:, 0:2 * FH], rf[:, 0:2 * FH]).then_inc(S["rec_set"], 1)
            e.wait_ge(S["rec_set"], 5)
            e.wait_ge(S["fo_mm"], FH)
            for m in range(NM):
                e.tensor_tensor(tok[:, m, 512:1024].rearrange("p (h d) -> p h d", h=FH),
                                ps[:, m, :].rearrange("p (h d) -> p h d", h=FH),
                                rrec[:, FH * m:FH * m + FH].unsqueeze(2).broadcast_to([P, FH, DH]), ALU.mult
                                ).then_inc(S["fo_ev"], 1)

            def hv(b, n=P, w=P):
                return ps[0:n, b, 0:GH * w].rearrange("p (h c) -> p h c", h=GH)

            def bc(col, n, w):
                return col.unsqueeze(2).broadcast_to([n, GH, w])
            for i, dst in enumerate((q_t[:, 0], q_t[:, 1], k_t[:, 0], k_t[:, 1])):
                e.wait_ge(S["gt_mm"], i + 1)
                e.tensor_copy(dst, hv(i)).then_inc(S["gt_d"], 1)
            for i in range(3):
                n = P if i < 2 else META
                src = k_t[:, i] if i < 2 else kv_m[:, 0]
                e.wait_ge(*((S["gt_d"], 3 + i) if i < 2 else (S["gt_a"], 3)))
                dst = junk[0:n, 8 + 4 * i:12 + 4 * i, :]
                e.tensor_tensor(dst, src, src, ALU.mult).then_inc(S["nk_sq"], 1)
                e.wait_ge(S["nk_sq"], 2 * i + 1)
                e.tensor_reduce(nrm[0:n, 0, 1, (i + 1) % 3, :], dst, AX_X, ALU.add).then_inc(S["nk_sq"], 1)
            e.wait_ge(S["nrm_sq"], NM * GH + 2)
            e.reciprocal(nrm[:, 2], nrm[:, 1]).then_inc(S["nrm_a"], 2)
            e.wait_ge(S["nrm_a"], 2)
            e.wait_ge(S["gs_set"], 2)
            rq, rk = nrm[:, 2, 0], nrm[:, 2, 1]
            e.tensor_tensor(coef[:, 0], rk, beta[:, :, :], ALU.mult).then_inc(S["coef_d"], 1)
            e.tensor_tensor(coef[:, 2], rk, EG[:, :, 4:8], ALU.mult).then_inc(S["coef_d"], 1)
            e.wait_ge(S["coef_d"], 1)
            e.tensor_tensor(coef[:, 1], coef[:, 0], EG[:, :, 0:4], ALU.mult).then_inc(S["coef_d"], 1)
            e.tensor_tensor(coef[:, 3], rq, EG[:, :, 0:4], ALU.mult).then_inc(S["coef_d"], 1)
            e.wait_ge(S["coef_d"], 4)
            e.wait_ge(S["gt_d"], 4)

            def scaled(m):
                for dst, src, c in ((Kn, k_t, rk), (Kb, k_t, coef[:, 0]), (Qn, q_t, rq), (Qg, q_t, coef[:, 3])):
                    e.tensor_tensor(dst[:, m], src[:, m], bc(c[:, 1 + m, :], P, P), ALU.mult).then_inc(S["sc_d"], 1)
            scaled(0)
            e.wait_ge(S["gt_a"], 3)
            e.tensor_tensor(Knm[:, :, :], kv_m[:, 0], bc(rk[0:META, 0, :], META, P), ALU.mult).then_inc(S["sc_d"], 1)
            e.tensor_tensor(Kbm[:, :, :], kv_m[:, 0], bc(coef[0:META, 0, 0, :], META, P), ALU.mult).then_inc(S["sc_d"], 1)
            scaled(1)
            e.wait_ge(S["tt_mm"], 1)
            e.tensor_copy(KnT[:, 0], hv(0)).then_inc(S["tt_d"], 1)
            e.wait_ge(S["tt_mm"], 3)
            e.tensor_copy(QnT[:, 0], hv(2)).then_inc(S["tt_d"], 1)
            e.wait_ge(S["tt_mm"], 5)
            e.tensor_copy(KnTm, hv(4, P, META)).then_inc(S["tt_d"], 1)
            e.tensor_copy(KbTm, ps[:, 4, 64:128].rearrange("p (h c) -> p h c", h=GH)).then_inc(S["tt_d"], 1)
            e.wait_ge(S["tt_mm"], 6)
            e.tensor_copy(KnT[:, 1], hv(0)).then_inc(S["tt_d"], 1)
            e.wait_ge(S["tt_mm"], 8)
            e.tensor_copy(QnT[:, 1], hv(2)).then_inc(S["tt_d"], 1)
            for i in range(4):
                e.wait_ge(S["kk_mm"], i + 1)
                e.wait_ge(S["e_set"], i // 2 + 1)
                e.tensor_tensor((AT, PT)[i % 2][:, i // 2], hv(i), E_[:, i // 2], ALU.mult).then_inc(S["at_d"], 1)
            e.wait_ge(S["kk_mm"], 5)
            e.wait_ge(S["e_set"], 3)
            e.tensor_tensor(ATm[0:META], hv(4, META, META), Em[0:META], ALU.mult).then_inc(S["at_d"], 1)
            for g in range(3):
                e.wait_ge(S["al_p"], g + 1)
                if g < 2:
                    e.tensor_tensor(TT_[:, g], ident[:, :].unsqueeze(1).broadcast_to([P, GH, P]), Al[:, g],
                                    ALU.subtract).then_inc(S["t0_set"], 1)
                else:
                    e.tensor_tensor(TTm[0:META], ident[0:META, 0:META].unsqueeze(1).broadcast_to([META, GH, META]),
                                    Alm[0:META], ALU.subtract).then_inc(S["t0_set"], 1)
            for lv in range(1, 7):
                for g in groups(lv):
                    e.wait_ge(S["z_mm"], count(lv, g) + 1)
                    if g < 2:
                        last = e.tensor_tensor(TT_[:, g], TT_[:, g], hv(6 + g), ALU.subtract)
                        if lv < 6:
                            last = e.tensor_tensor(T_[:, g], T_[:, g], hv(3 + g), ALU.subtract)
                    else:
                        e.tensor_tensor(TTm[0:META], TTm[0:META],
                                        ps[0:META, 5, 64:128].rearrange("p (h c) -> p h c", h=GH), ALU.subtract)
                        last = e.tensor_tensor(Tm[0:META], Tm[0:META], hv(5, META, META), ALU.subtract)
                    last.then_inc(S["t_up"], 1)
            for m in range(NM):
                e.wait_ge(S["uw_mm"], 4 + m)
                e.tensor_copy(wT[:, m], hv(2 + m)).then_inc(S["w_ev"], 1)
            e.wait_ge(S["s1_mm"], 1)
            e.tensor_copy(Sst, hv(5)).then_inc(S["s_set"], 1)
            for m in range(NM):
                e.wait_ge(S["ws_mm"], m + 1)
                e.wait_ge(S["u_ev"], m + 2)
                e.tensor_tensor(vn, u[:, m], hv(6), ALU.subtract).then_inc(S["vn_set"], 1)
                if m == 0:
                    e.wait_ge(S["ds_mm"], 1)
                    e.wait_ge(S["s_set"], 1)
                    for h in range(GH):
                        e.scalar_tensor_tensor(out=Sst[:, h, :], in0=Sst[:, h, :], scalar=EG[:, 1, 8 + h:9 + h],
                                               in1=ps[:, 7, P * h:P * h + P], op0=ALU.mult, op1=ALU.add
                                               ).then_inc(S["s_set"], 1)
            e.wait_ge(S["oz_set"], 2)
            for m in range(NM):
                e.wait_ge(S["on_sq"], 5 * m + 5)
                e.reciprocal(onrm[:, 2, m, :], onrm[:, 1, m, :]).then_inc(S["on_set"], 1)
                e.wait_ge(S["on_set"], m + 1)
                v = tok[:, m, 0:512]
                e.tensor_tensor(v.rearrange("p (h d) -> p h d", h=GH), hv(m), bc(onrm[:, 2, m, :], P, P), ALU.mult
                                ).then_inc(S["og_set"], 1)
                e.wait_ge(S["og_set"], 2 * m + 1)
                e.tensor_tensor(v, v, zs[:, m, :], ALU.mult).then_inc(S["og_set"], 1)
                if m == 0:
                    split(T_WOUT, landed(N_WOUT)[0])

            def residual2(i, done, then):
                for m in range(NM):
                    for c in range(2):
                        e.wait_ge(*done[2 * m + c])
                        xc = x[:, m, 512 * c:512 * c + 512]
                        e.tensor_tensor(xc, xc, ps[:, 2 * m + c, :], ALU.add).then_inc(S["r2_add"], 1)
                        if (m, c) == (1, 0):
                            then(0)
                then(1)
            split_h()
            split(T_WOUT + 1, landed(N_WOUT + 1)[0])
            residual2(0, [(y, 11), (y, 12), (used, 2 * T_WOUT + 2), (used, 2 * T_WOUT + 4)], normalise_tile)
            split(T_FFN, N_FFN % R, qs=(0, 1))
            split_h()
            split(T_FFN, N_FFN % R, qs=(2, 3))

            def g_mul(j):
                for m in range(NM):
                    e.wait_ge(S["gr_done"], 2 * j + m + 1)
                    e.tensor_tensor(act[:, m, 0:256], relu[:, m, 0:256], ps[:, 4 + m, 256:512], ALU.mult
                                    ).then_inc(S["ga_done"], 1)

            def g_aT(j):
                e.wait_ge(S["gth_done"], j + 1)
                e.tensor_tensor(aTl[:, 0:2, :], ps[:, 6, :].rearrange("p (k t) -> p k t", k=2),
                                aTh[:, 0:2, :].bitcast(F32), ALU.subtract).then_inc(S["gtl_done"], 1)
            split(T_FFN + 1, (N_FFN + 1) % R, qs=(0, 1))
            g_mul(0)
            split(T_FFN + 1, (N_FFN + 1) % R, qs=(2, 3))
            g_aT(0)

            def g_body(i, last=False):
                for r in range(2):
                    split(T_FFN + 2 + 2 * r + 4 * i, (N_FFN + 2 + 2 * r) % R, words=HALF)
                    g_mul(1 + r + 2 * i)
                    if not (last and r):
                        split(T_FFN + 3 + 2 * r + 4 * i, (N_FFN + 3 + 2 * r) % R)
                    g_aT(1 + r + 2 * i)
            with e.Fori(0, 4) as i:
                g_body(i)
            g_body(4, last=True)
            split(T_FFN + 21, (N_FFN + 21) % R, words=HALF)
            def second_output(m):
                if m == 0:
                    e.wait_ge(S["row_in"], 32)
                rstd(m)
                e.scalar_tensor_tensor(out=tok[:, m, :], in0=x[:, m, :], scalar=stat[:, 2, m:m + 1], in1=gate[1][:, :],
                                       op0=ALU.mult, op1=ALU.mult).then_inc(S["fin_set"], 1)
            residual2(1, [(y, 13), (y, 14), (y, 15), (used, 2 * (T_FFN + 22))], second_output)

        @block.tensor
        def _(e):
            e.wait_ge(S["made"], 7)
            e.wait_ge(S["c_in"], 16)
            e.transpose(ps[:, 7, 256:264], prow[0:8, 1, :], ident[0:8, 0:8]).then_inc(S["ptr"], 1)
            e.wait_ge(S["par_in"], 112)
            e.wait_ge(S["cc_set"], 1)
            e.transpose(ps[:, 7, 0:P], prow[:, 0, :], ident[:, :])
            e.transpose(ps[:, 7, P:P + 80], prow[0:80, 1, :], ident[0:80, 0:80]).then_inc(S["ptr"], 1)
            e.wait_ge(S["rb_in"], 16)
            e.wait_ge(S["oh_in"], 16)
            e.matmul(ps[0:HEADS, 6, 0:NDIST], rb[:, :], oh[:, :], start=True, stop=True).then_inc(S["f_mm"], 1)

            def mod_mm(u):
                n = MOD0_LOADS[u]
                e.wait_ge(raw_in[n % R], landed(n)[1])
                if u:
                    e.wait_ge(S["mod_col"], u)
                w = kview(n % R)
                for c in range(4):
                    for k in range(MOD0_PE[u]):
                        e.matmul(ps[:, 2, c:c + 1], w[:, k, P * c:P * c + P], ccol[:, 0, k:k + 1],
                                 start=(c == 0 and k == 0), stop=False)
                e.wait_ge(S["mod_acc"], u + 1)
                for c in range(4):
                    ins = e.matmul(ps[:, 2, c:c + 1], acc[:, u % 2, P * c:P * c + P], ones[:, 0:1],
                                   start=False, stop=(c == 3))
                ins.then_inc(S["mod_mm"], 1)
            e.wait_ge(S["c_s"], 3)
            mod_mm(0)
            mod_mm(1)

            ntr = [0]
            nx = [0]

            def feature_major(ready, free=()):
                for s, v in free:
                    e.wait_ge(s, v)
                for m in range(NM):
                    e.wait_ge(*ready[m])
                    for k in range(KD):
                        ins = e.transpose(ps[:, 4 + k // 2, (k % 2) * SEQ + P * m:(k % 2) * SEQ + P * m + P],
                                          tok[:, m, P * k:P * k + P], ident[:, :])
                        if m == 1 and k % 2:
                            ins.then_inc(S["tr_done"], 1)

            def xn_ready():
                i = nx[0]
                nx[0] += 1
                return [(S["xn_done"], 2 * i + 1), (S["xn_done"], 2 * i + 2)]

            ng = [0]

            fresh = [None]

            def parts(k):
                if fresh[0] is not None and k % 2 == 0:
                    e.wait_ge(S["hs_l"], fresh[0] + k // 2 + 1)
                    if k == KD - 2:
                        fresh[0] = None

            def rows_half(hb, b, name, src=(H, L)):
                w = [q[:, hb, :].rearrange("p (k n) -> p k n", k=4) for q in (wh, wl)]
                for m in range(NM):
                    bank = b(m) if callable(b) else b + m
                    for k in range(4):
                        parts(4 * hb + k)
                        for n, (xa, wb) in enumerate(PASSES):
                            ins = e.matmul(ps[:, bank, :], src[xa][:, 4 * hb + k, META + P * m:META + P * m + P],
                                           w[wb][:, k, :], start=(hb == 0 and k == 0 and n == 0),
                                           stop=(hb == 1 and k == 3 and n == 2))
                    if hb == 1 and m == 0:
                        ins.then_inc(S[name], 1)
                return ins

            def wo_out(t):
                for c in range(2):
                    for hb in range(2):
                        half(t + c, hb)
                        rows_half(hb, lambda m: 2 * m + c, "y_done").then_inc(S["split_used"], 1)

            def gate_mm(b=0):
                i = ng[0]
                ng[0] += 1
                for k in range(KD):
                    e.wait_ge(S["gate_diag"], 8 * i + k + 1)
                    ins = e.matmul(ps[:, b + k // 4, P * (k % 4):P * (k % 4) + P], ones[:, :], diag[:, k, :],
                                   start=True, stop=True)
                    if k % 4 == 3:
                        ins.then_inc(S["gate_mm"], 1)

            def half(t, hb):
                e.wait_ge(S["split_l"], 4 * t + 2 * hb + 2)

            def up(it, t, mods_in=None):
                for hb in range(2):
                    half(t, hb)
                    w = [q[:, hb, :].rearrange("p (k n) -> p k n", k=4) for q in (wh, wl)]
                    for m in range(NM):
                        if hb == 0 and not (isinstance(it, int) and it == 0):
                            e.wait_ge(S["r_done"], 2 * it - 1 + m)
                        if hb == 0 and m == 1 and mods_in is not None:
                            e.wait_ge(S["mod_col"], mods_in)
                        for k in range(4):
                            parts(4 * hb + k)
                            for n, (xa, wb) in enumerate(PASSES):
                                ins = e.matmul(ps[:, 4 + m, :], (H, L)[xa][:, 4 * hb + k, META + P * m:META + P * m + P],
                                               w[wb][:, k, :], start=(hb == 0 and k == 0 and n == 0),
                                               stop=(hb == 1 and k == 3 and n == 2))
                        if hb == 1 and m == 0:
                            ins.then_inc(S["u_done"], 1)
                    ins.then_inc(S["split_used"], 1)

            def turn(it):
                e.wait_ge(S["a_done"], 2 * it + 2)
                if not (isinstance(it, int) and it == 0):
                    e.wait_ge(S["tl_done"], 2 * it)
                for k in range(4):
                    for m in range(NM):
                        ins = e.transpose(ps[:, 6 + k // 2, (k % 2) * SEQ + P * m:(k % 2) * SEQ + P * m + P],
                                          act[:, m, P * k:P * k + P], ident[:, :])
                    if k % 2:
                        ins.then_inc(S["t_done"], 1)

            def down(it, t, last=False):
                e.wait_ge(S["tl_done"], 2 * it + 2)
                for hb in range(2):
                    half(t, hb)
                    w = [q[:, hb, :].rearrange("p (k n) -> p k n", k=2) for q in (wh, wl)]
                    for m in range(NM):
                        for c in range(2):
                            for k in range(2):
                                for n, (xa, wb) in enumerate(PASSES):
                                    ins = e.matmul(ps[:, 2 * m + c, :], (aTh, aTl)[xa][:, 2 * hb + k, P * m:P * m + P],
                                                   w[wb][:, k, 512 * c:512 * c + 512], start=False,
                                                   stop=(last and hb == 1 and k == 1 and n == 2))
                            if last and hb == 1 and 2 * m + c < 3:
                                ins.then_inc(S["y_done"], 1)
                    ins.then_inc(S["split_used"], 1)

            def open_y(*ready):
                e.wait_ge(*ready)
                for b in range(4):
                    e.matmul(ps[:, b, :], zrow[:, :], zrow[:, 0:1].broadcast_to([1, 512]), start=True, stop=False)

            feature_major(xn_ready(), [(S["f_sb"], 1), (S["pcopied"], 2)])
            for u in range(2, 5):
                mod_mm(u)
            for g in range(4):
                if g % 2 == 0:
                    half(T_POOL, g // 2)
                e.wait_ge(S["hs_l"], g + 1)
                for m in range(NM):
                    for k in range(2):
                        for n, (xa, wb) in enumerate(PASSES):
                            w = (wh, wl)[wb][:, g // 2, 0:HALF // 2].rearrange("p (g k n) -> p g k n", g=2, k=2)
                            ins = e.matmul(ps[:, 4 + 2 * m + g // 2, 256 * (g % 2):256 * (g % 2) + 256],
                                           (H, L)[xa][:, 2 * g + k, META + P * m:META + P * m + P],
                                           w[:, g % 2, k, :], start=(k == 0 and n == 0), stop=(k == 1 and n == 2))
                    if g % 2 and not (g == 1 and m == 1) and not (g == 3 and m == 1):
                        ins.then_inc(S["y_done"], 1)
                if g % 2:
                    ins.then_inc(S["split_used"], 1)
                if g == 1:
                    mod_mm(5)
            gate_mm()
            for u in range(6, 10):
                mod_mm(u)
            e.wait_ge(S["res_mul"], 4)
            feature_major(xn_ready())
            e.wait_ge(S["gate_set"], 2)
            open_y(S["mod_col"], 10)
            fresh[0] = 4
            up(0, T_MLP0)
            turn(0)
            up(1, T_MLP0 + 1)
            down(0, T_MLP0 + 2)
            e.wait_ge(S["r_done"], 4)
            e.wait_ge(S["mod_acc"], 11)
            e.wait_ge(S["mod_accb"], 1)
            for c in range(8):
                ins = e.matmul(ps[:, 5, c:c + 1], acc[:, c // 4, P * (c % 4):P * (c % 4) + P], ones[:, 0:1],
                               start=True, stop=True)
            ins.then_inc(S["mod_mm"], 2)
            turn(1)
            with e.Fori(2, 8) as j:
                up(j, T_MLP0 - 1 + 2 * j, 10 + j)
                down(j - 1, T_MLP0 + 2 * j)
                e.wait_ge(S["r_done"], 2 * j + 2)
                e.wait_ge(S["mod_acc"], 10 + j)
                e.wait_ge(S["mod_accb"], j)
                for c in range(4):
                    ins = e.matmul(ps[:, 5, c:c + 1], acc[:, c // 2, P * (c % 2):P * (c % 2) + P], ones[:, 0:1],
                                   start=True, stop=True)
                ins.then_inc(S["mod_mm"], 1)
                turn(j)
            e.wait_ge(S["mod_col"], 18)
            gate_mm(4)
            down(7, T_MLP0 + 15, last=True)
            e.wait_ge(S["gate_set"], 4)
            feature_major(xn_ready())
            e.wait_ge(S["res_mul"], 8)
            fresh[0] = 8
            for i in range(6):
                t = T_QKV + i
                b = 2 * (i % 4)
                if i >= 4:
                    e.wait_ge(S["ev_act"], i - 3)
                    e.wait_ge(S["ev_dve"], i - 3)
                for hb in range(2):
                    half(t, hb)
                    if i < 4:
                        w = [q[:, hb, :].rearrange("p (k n) -> p k n", k=KD) for q in (wh, wl)]
                        for c in range(2):
                            for k in range(KD):
                                parts(k)
                                for n, (xa, wb) in enumerate(PASSES):
                                    ins = e.matmul(ps[:, b + hb, SEQ * c:SEQ * c + SEQ], w[wb][:, k, P * c:P * c + P],
                                                   (H, L)[xa][:, k, META:TT], start=(k == 0 and n == 0),
                                                   stop=(k == KD - 1 and n == 2))
                    else:
                        ins = rows_half(hb, b, "qkv_mm")
                    ins.then_inc(S["split_used"], 1)
            e.wait_ge(S["ev_act"], 6)
            e.wait_ge(S["ev_dve"], 6)
            def scores(h):
                p0, blk = DH * (h % 2), h // 2
                if h >= 4:
                    e.wait_ge(S["t_set"], 2 * (h - 4) + 2)
                e.matmul(ps[:, 4 + h % 4, 0:SEQ], qT[p0:p0 + DH, blk, P:SEQ], kT[p0:p0 + DH, blk, :],
                         start=True, stop=True)
                e.matmul(ps[:, 4 + h % 4, SEQ:SEQ + P], qT[p0:p0 + DH, blk, 0:P], kT[p0:p0 + DH, blk, 0:P],
                         start=True, stop=True).then_inc(S["s_mm"], 1)
            def unit_sum(u):
                e.wait_ge(S["t_set"], 2 * 12 + 2)
                e.wait_ge(S["mod_accu"], u + 1)
                for c in range(3 * u, 3 * u + 3):
                    ins = e.matmul(ps[:, 4, c:c + 1], accu[:, u, P * (c % 3):P * (c % 3) + P], ones[:, 0:1],
                                   start=True, stop=True)
                return ins
            scores(0)
            scores(1)
            for h in range(HEADS + 2):
                if h + 2 < HEADS:
                    scores(h + 2)
                for u in {HEADS - 2: (0, 1), HEADS - 1: (2, 3), HEADS: (4, 5), HEADS + 1: (6,)}.get(h, ()):
                    unit_sum(u)
                g = h - 1
                if 0 <= g < HEADS:
                    e.wait_ge(S["p_set"], 2 * g + 2)
                    if g >= 2:
                        e.wait_ge(S["pt_ev"], g - 1)
                    for c in range(3):
                        ins = e.transpose(ps[:, 2 + g % 2, P * c:P * c + P], P_sc[:, g % 2, P * c:P * c + P], ident[:, :])
                    ins.then_inc(S["pt_mm"], 1)
                g = h - 2
                if g >= 0:
                    e.wait_ge(S["pt_ev"], g + 1)
                    if g >= 8 and g % 4 == 0:
                        e.wait_ge(S["o_ev"], g // 4 - 1)
                    o = ps[:, (g // 4) % 2, :].rearrange("p (m h d) -> p m h d", m=2, h=4)
                    vv = v_tok[:, :, DH * g:DH * g + DH]
                    e.matmul(o[:, 0, g % 4, :], PT_sc[:, g % 2, 256:384], vv[:, 0, :], start=True, stop=True)
                    e.matmul(o[:, 1, g % 4, :], PT_sc[:, g % 2, 0:128], vv[:, 0, :], start=True, stop=False)
                    e.matmul(o[:, 1, g % 4, :], PT_sc[:, g % 2, 128:256], vv[:, 1, :], start=False, stop=True
                             ).then_inc(S["o_mm"], 1)
            unit_sum(NMU - 1).then_inc(S["mod_mm"], 1)
            e.wait_ge(S["mod_col"], 19)
            feature_major([(S["o_ev"], 4)] * 2)
            gate_mm()
            e.wait_ge(S["gate_set"], 6)
            gate_mm()
            e.wait_ge(S["gate_set"], 8)
            fresh[0] = 12
            wo_out(T_WO)
            feature_major(xn_ready())
            open_y(S["res_mul"], 12)
            fresh[0] = 16
            up(8, T_MLP1)
            turn(8)
            with e.Fori(0, 3) as i:
                for r in range(2):
                    up(9 + 2 * i + r, T_MLP1 + 1 + 4 * i + 2 * r)
                    down(8 + 2 * i + r, T_MLP1 + 2 + 4 * i + 2 * r)
                    turn(9 + 2 * i + r)
            up(15, T_MLP1 + 13)
            down(14, T_MLP1 + 14)
            turn(15)
            down(15, T_MLP1 + 15, last=True)
            feature_major(xn_ready())
            e.wait_ge(S["xnm_done"], 1)
            e.wait_ge(S["res_mul"], 16)
            for k in range(KD):
                ins = e.transpose(ps[:, 3, META * k:META * k + META], tokm[:, P * k:P * k + P], ident[0:META, 0:META])
            ins.then_inc(S["mtr_done"], 1)
            e.wait_ge(S["hfm_done"], 1)
            e.wait_ge(S["hf_done"], 8 * 6)
            e.wait_ge(S["wsm_in"], 32)
            tiles = [(0, META), (META, P), (META + P, P)]
            for s, (t0, w) in enumerate(tiles):
                for k in range(KD):
                    ins = e.matmul(ps[0:w, 3, 256 + 16 * s:272 + 16 * s], hf[:, k, t0:t0 + w], wsm[:, k, :],
                                   start=(k == 0), stop=(k == KD - 1))
            ins.then_inc(S["sm_mm"], 1)
            fresh[0] = 20
            for i in range(7):
                t = T_WIN + i
                b = 4 if i % 2 == 0 else 0
                if i == 1:
                    e.wait_ge(S["sm_set"], 2)
                if i >= 2:
                    e.wait_ge(S["pj_ev"], (4, 8, 12, 14, 18)[i - 2])
                for hb in range(2):
                    half(t, hb)
                    if i == 3:
                        ins = rows_half(hb, 0, "pj_mm")
                    else:
                        w = [q[:, hb, :].rearrange("p (k n) -> p k n", k=KD) for q in (wh, wl)]
                        for c in range(2):
                            for k in range(KD):
                                parts(k)
                                for n, (xa, wb) in enumerate(PASSES):
                                    ins = e.matmul(ps[:, b + 2 * hb + c, 0:TT], w[wb][:, k, P * c:P * c + P],
                                                   (H, L)[xa][:, k, :], start=(k == 0 and n == 0),
                                                   stop=(k == KD - 1 and n == 2))
                            if c == 0:
                                ins.then_inc(S["pj_mm"], 1)
                    ins.then_inc(S["split_used"], 1)
            e.wait_ge(S["pj_ev"], 26)
            e.wait_ge(S["tk_d"], 8)
            e.wait_ge(S["made2"], 9)
            tri = wtri[:, META + P:META + 2 * P]
            for s, (v0, w) in enumerate(((META + P, META), (P, P), (0, P))):
                ins = e.matmul(ps[0:FH, 0, 0:TT], tks[0:w, 1, s, 4:12], wtri[0:w, v0:v0 + TT], start=(s == 0), stop=(s == 2))
            ins.then_inc(S["nc_mm"], 1)
            for s in range(NM):
                for c, lhs in enumerate((tri, masks[:, 7, :], ones[:, :])):
                    ins = e.matmul(ps[:, 1, 12 * s + 4 * c:12 * s + 4 * c + 4], lhs, gdec[:, 1 + s, :], start=True, stop=True)
            ins.then_inc(S["gs_mm"], 1)
            e.matmul(ps[0:META, 2, 0:4], masks[0:META, 7, 0:META], gdec[0:META, 0, :], start=True, stop=True
                     ).then_inc(S["gs_mm"], 1)
            e.wait_ge(S["nc_set"], 1)
            for h in range(FH):
                if h >= 2:
                    e.wait_ge(S["cm_raw"], h - 1)
                e.matmul(ps[:, (3, 0)[h % 2], 0:TT], ident[0:FH, h:h + 1].broadcast_to([FH, P]), ncT, start=True, stop=True
                         ).then_inc(S["bc_mm"], 1)
            def fox_scores(h):
                    p0, blk = DH * (h % 2), h // 2
                    if h >= 2:
                        e.wait_ge(S["ft_set"], 2 * (h - 2) + 2)
                    q, k = fT[p0:p0 + DH, blk, :], fT[p0:p0 + DH, 4 + blk, :]
                    e.matmul(ps[:, 4 + h % 2, 0:TT], q[:, META + P:TT], k, start=True, stop=True)
                    e.matmul(ps[:, 4 + h % 2, TT:TT + META + P], q[:, META:META + P], k[:, 0:META + P],
                             start=True, stop=True).then_inc(S["fs_mm"], 1)
            fox_scores(0)
            fox_scores(1)
            e.wait_ge(S["gs_set"], 2)
            for i, (b, t0, w) in enumerate(((6, META, P), (7, META + P, P), (2, 0, META))):
                for c in range(4):
                    ins = e.transpose(ps[0:w, b, P * c:P * c + P], fT[:, 8 + c, t0:t0 + w], ident[:, :])
                ins.then_inc(S["vt_mm"], 1)
            e.wait_ge(S["cm_raw"], FH)
            for h in range(FH + 2):
                if 2 <= h < FH:
                    fox_scores(h)
                g = h - 1
                if 0 <= g < FH:
                    e.wait_ge(S["fp_set"], 2 * g + 2)
                    if g == 0:
                        e.wait_ge(S["vt_ev"], 2)
                        e.wait_ge(S["vtm_ev"], 1)
                    if g >= 2:
                        e.wait_ge(S["fpa_ev"], g - 1)
                        e.wait_ge(S["fpb_ev"], g - 1)
                    Pg = P_f[:, g % 2, :]
                    for c, c0 in enumerate((META, META + P, TT + META)):
                        e.transpose(ps[:, 2 + g % 2, P * c:P * c + P], Pg[:, c0:c0 + P], ident[:, :])
                    for c, c0 in enumerate((0, TT)):
                        ins = e.transpose(ps[0:META, 6 + g % 2, P * c:P * c + P], Pg[:, c0:c0 + META], ident[:, :])
                    ins.then_inc(S["fpt_mm"], 1)
                g = h - 2
                if g >= 0:
                    e.wait_ge(S["fpa_ev"], g + 1)
                    e.wait_ge(S["fpb_ev"], g + 1)
                    c = slice(DH * g, DH * g + DH)
                    a_, b_ = PTa[:, g % 2, :], PTb[:, g % 2, :]
                    e.matmul(ps[:, 0, c], b_[:, P:2 * P], vtm[:, c], start=True, stop=False)
                    e.matmul(ps[:, 0, c], a_[:, 2 * P:3 * P], vt[:, 0, c], start=False, stop=True)
                    e.matmul(ps[:, 1, c], b_[:, 0:P], vtm[:, c], start=True, stop=False)
                    e.matmul(ps[:, 1, c], a_[:, 0:P], vt[:, 0, c], start=False, stop=False)
                    e.matmul(ps[:, 1, c], a_[:, P:2 * P], vt[:, 1, c], start=False, stop=True).then_inc(S["fo_mm"], 1)
            e.wait_ge(S["fo_ev"], 2)
            e.wait_ge(S["silu_set"], 4)
            for b, (blk, t0, w) in enumerate(((0, META, P), (0, META + P, P), (4, META, P), (4, META + P, P),
                                              (8, META, P), (8, META + P, P), (4, 0, META), (8, 0, META))):
                for h in range(GH):
                    ins = e.transpose(ps[0:w, b, P * h:P * h + P], yT[:, blk + h, t0:t0 + w], ident[:, :])
                ins.then_inc(S["gt_mm"], 1)
            e.wait_ge(S["gt_a"], 4)
            for g in range(3):
                e.wait_ge(S["dl_p"], g + 1)
                for h in range(GH):
                    if g < 2:
                        ins = e.matmul(ps[:, 6 + g, P * h:P * h + P], DL[:, g, h, :], tri, start=True, stop=True)
                    else:
                        ins = e.matmul(ps[0:META, 5, META * h:META * h + META], DLm[0:META, h, :],
                                       tri[0:META, 0:META], start=True, stop=True)
                ins.then_inc(S["d_mm"], 1)

            def turned(m):
                for b, src in enumerate((Kn, Kb, Qn, Qg)):
                    e.wait_ge(S["sc_d"], b + 1 + 6 * m)
                    if m:
                        e.wait_ge(*((S["tt_d"], b // 2 + 1) if b % 2 == 0 else (S["tt_a"], b // 2 + 1)))
                    for h in range(GH):
                        ins = e.transpose(ps[:, b, P * h:P * h + P], src[:, m, h, :], ident[:, :])
                    ins.then_inc(S["tt_mm"], 1)
            turned(0)
            e.wait_ge(S["sc_d"], 6)
            for i, src in enumerate((Knm, Kbm)):
                for h in range(GH):
                    ins = e.transpose(ps[:, 4, 64 * i + META * h:64 * i + META * h + META], src[:, h, :],
                                      ident[0:META, 0:META])
            ins.then_inc(S["tt_mm"], 1)
            turned(1)
            e.wait_ge(S["tt_d"], 6)
            e.wait_ge(S["tt_a"], 4)
            for i in range(4):
                m = i // 2
                for h in range(GH):
                    ins = e.matmul(ps[:, i, P * h:P * h + P], KnT[:, m, h, :], (KbT, QnT)[i % 2][:, m, h, :],
                                   start=True, stop=True)
                ins.then_inc(S["kk_mm"], 1)
            for h in range(GH):
                ins = e.matmul(ps[0:META, 4, META * h:META * h + META], KnTm[:, h, :], KbTm[:, h, :], start=True, stop=True)
            ins.then_inc(S["kk_mm"], 1)
            for g in range(3):
                e.wait_ge(S["t0_set"], g + 1)
                for h in range(GH):
                    if g < 2:
                        ins = e.transpose(ps[:, g, P * h:P * h + P], TT_[:, g, h, :], ident[:, :])
                    else:
                        ins = e.transpose(ps[0:META, 2, META * h:META * h + META], TTm[0:META, h, :], ident[0:META, 0:META])
                ins.then_inc(S["t0_mm"], 1)
            for lv in range(1, 7):
                for g in groups(lv):
                    e.wait_ge(S["al_p"], 3 + count(lv, g) + 1)
                    e.wait_ge(*((S["t0_ev"], g + 1) if lv == 1 else (S["t_up"], count(lv - 1, g) + 1)))
                    if lv > 1:
                        e.wait_ge(S["x_ev"], count(lv - 1, g) + 1)
                    for h in range(GH):
                        if g < 2:
                            ins = e.matmul(ps[:, g, P * h:P * h + P], Al[:, g, h, :], T_[:, g, h, :], start=True, stop=True)
                        else:
                            ins = e.matmul(ps[0:META, 2, META * h:META * h + META], Alm[0:META, h, :], Tm[0:META, h, :],
                                           start=True, stop=True)
                    ins.then_inc(S["x_mm"], 1)
                for g in groups(lv):
                    e.wait_ge(S["x_ev"], count(lv, g) + 1)
                    for h in range(GH):
                        if g < 2:
                            if lv < 6:
                                e.matmul(ps[:, 3 + g, P * h:P * h + P], TT_[:, g, h, :], X[:, g, h, :], start=True, stop=True)
                            ins = e.matmul(ps[:, 6 + g, P * h:P * h + P], X[:, g, h, :], TT_[:, g, h, :], start=True, stop=True)
                        else:
                            c = slice(META * h, META * h + META)
                            e.matmul(ps[0:META, 5, c], TTm[0:META, h, :], Xm[0:META, h, :], start=True, stop=True)
                            c = slice(64 + META * h, 64 + META * h + META)
                            ins = e.matmul(ps[0:META, 5, c], Xm[0:META, h, :], TTm[0:META, h, :], start=True, stop=True)
                    ins.then_inc(S["z_mm"], 1)
            e.wait_ge(S["t_up"], count(7, 0))
            e.wait_ge(S["sc_p"], 8)
            for h in range(GH):
                ins = e.matmul(ps[0:META, 4, P * h:P * h + P], TTm[0:META, h, :], R1m[:, h, :], start=True, stop=True)
            ins.then_inc(S["uw_mm"], 1)
            for m in range(NM):
                for h in range(GH):
                    ins = e.matmul(ps[:, m, P * h:P * h + P], TT_[:, m, h, :], R1[:, m, h, :], start=True, stop=True)
                ins.then_inc(S["uw_mm"], 1)
            for m in range(NM):
                for h in range(GH):
                    ins = e.matmul(ps[:, 2 + m, P * h:P * h + P], R2[:, m, h, :], TT_[:, m, h, :], start=True, stop=True)
                ins.then_inc(S["uw_mm"], 1)
            e.wait_ge(S["u_ev"], 1)
            for h in range(GH):
                ins = e.matmul(ps[:, 5, P * h:P * h + P], Kdm[:, h, :], um[:, h, :], start=True, stop=True)
            ins.then_inc(S["s1_mm"], 1)
            for m in range(NM):
                e.wait_ge(S["s_set"], 1 + 4 * m)
                e.wait_ge(S["w_ev"], m + 1)
                for h in range(GH):
                    ins = e.matmul(ps[:, 6, P * h:P * h + P], wT[:, m, h, :], Sst[:, h, :], start=True, stop=True)
                ins.then_inc(S["ws_mm"], 1)
                e.wait_ge(S["vn_set"], m + 1)
                e.wait_ge(S["at_p"], 4)
                for h in range(GH):
                    e.matmul(ps[:, m, P * h:P * h + P], QgT[:, m, h, :], Sst[:, h, :], start=True, stop=False)
                    ins = e.matmul(ps[:, m, P * h:P * h + P], PT[:, m, h, :], vn[:, h, :], start=False, stop=True)
                ins.then_inc(S["go_mm"], 1)
                if m == 0:
                    for h in range(GH):
                        ins = e.matmul(ps[:, 7, P * h:P * h + P], Kd[:, m, h, :], vn[:, h, :], start=True, stop=True)
                    ins.then_inc(S["ds_mm"], 1)
            feature_major([(S["og_set"], 2), (S["og_set"], 4)])
            fresh[0] = 24
            wo_out(T_WOUT)
            feature_major(xn_ready())
            open_y(S["r2_add"], 4)
            fresh[0] = 28

            def g_up(j, t):
                for m in range(NM):
                    if not (isinstance(j, int) and j == 0):
                        e.wait_ge(S["ga_done"], 2 * j - 1 + m)
                for hb in range(2):
                    half(t, hb)
                    rows_half(hb, 4, "gu_done").then_inc(S["split_used"], 1)

            def g_turn(j):
                e.wait_ge(S["ga_done"], 2 * j + 2)
                if not (isinstance(j, int) and j == 0):
                    e.wait_ge(S["gtl_done"], j)
                for k in range(2):
                    for m in range(NM):
                        ins = e.transpose(ps[:, 6, k * SEQ + P * m:k * SEQ + P * m + P], act[:, m, P * k:P * k + P],
                                          ident[:, :])
                ins.then_inc(S["gt_done"], 1)

            def g_down(j, t, last=False):
                e.wait_ge(S["gtl_done"], j + 1)
                for hb in range(2):
                    half(t, hb)
                    for m in range(NM):
                        for c in range(2):
                            for n, (xa, wb) in enumerate(PASSES):
                                ins = e.matmul(ps[:, 2 * m + c, :], (aTh, aTl)[xa][:, hb, P * m:P * m + P],
                                               (wh, wl)[wb][:, hb, 512 * c:512 * c + 512], start=False,
                                               stop=(last and hb == 1 and n == 2))
                            if last and hb == 1 and 2 * m + c < 3:
                                ins.then_inc(S["y_done"], 1)
                    ins.then_inc(S["split_used"], 1)
            g_up(0, T_FFN)
            g_turn(0)
            with e.Fori(0, 5) as i:
                for r in range(2):
                    g_up(1 + r + 2 * i, T_FFN + 1 + 2 * r + 4 * i)
                    g_down(r + 2 * i, T_FFN + 2 + 2 * r + 4 * i)
                    g_turn(1 + r + 2 * i)
            g_down(NJ2 - 1, T_FFN + 21, last=True)


_INS = ["x", "c", "rel_bias", "w_mod", "b_mod", "norm_mix", "norm_mlp", "w_pool", "pool_scale", "w_qkv", "w_o", "w_up",
        "w_down", "norm_final", "meta_tokens_2", "attn_norm_w_2", "w_in_2", "conv_w_2", "a_log_2", "dt_bias_2",
        "gdn_norm_w_2", "fgate_b_2", "w_out_2", "ffn_norm_w_2", "w_gate_2", "w_up_2", "w_down_2", "final_norm_w_2"]


def distance_rows():
    d = np.arange(NDIST) - (P - 1)
    half, far = BUCKETS // 2, 1024
    nf = np.maximum(d, 1).astype(np.float32)
    large = half + (np.log(nf / np.float32(half)) / np.float32(math.log(far / half)) * np.float32(half)).astype(np.int32)
    b = np.where(d < half, d, np.minimum(large, BUCKETS - 1))
    b = np.where(d < 0, BUCKETS, b)
    return (np.arange(BUCKETS + 1)[:, None] == b[None, :]).astype(np.float32)


def level_masks():
    i = np.arange(P)
    rows = []
    for lv in range(7):
        b = 2 ** lv
        same = i[:, None] // (2 * b) == i[None, :] // (2 * b)
        rows.append(same & (i[:, None] % (2 * b) < b) & (i[None, :] % (2 * b) >= b))
    return np.stack(rows, 1).astype(np.float32)


def kernel(**inputs):
    import concourse.bacc as bacc
    from concourse.bass_utils import run_bass_kernel_spmd

    nc = bacc.Bacc("TRN2", target_bir_lowering=False, num_devices=1)
    arrays = {name: np.ascontiguousarray(inputs[name]) for name in _INS}
    arrays["onehot"] = distance_rows()
    arrays["level_masks"] = level_masks()
    feeds, args = {}, {}
    for name, v in arrays.items():
        feeds[f"in_{name}"] = v
        args[name] = nc.dram_tensor(f"in_{name}", v.shape, mybir.dt.from_np(v.dtype), kind="ExternalInput").ap()
    out = nc.dram_tensor("out_0", (1, SEQ, D), F32, kind="ExternalOutput").ap()
    build(nc, args, out)
    r = run_bass_kernel_spmd(nc, [feeds], core_ids=[0])
    return r.results[0]["out_0"]
```
